# Optimizing a Trainium2 kernel written in Bass

```python
import math
import jax, jax.numpy as jnp
from jax import lax
import numpy as np

D_MODEL = 1024
BATCH = 1
SEQ = 512
DEPTH = 1
DEC_BATCH = 8
DEC_SEQ = 4
PAST_LEN = 1024
PAGE_SIZE = 128

HEAD_DIM = 64
CONV_CH = D_MODEL // 4
WINDOWS = (128, 512, 2048)
DILATIONS = (1, 4, 16)
N_DIL_GROUPS = len(WINDOWS)
HEADS_PER_GROUP = (D_MODEL - CONV_CH) // (N_DIL_GROUPS * HEAD_DIM)
N_ATTN_HEADS = N_DIL_GROUPS * HEADS_PER_GROUP
ATTN_WIDTH = N_ATTN_HEADS * HEAD_DIM
N_STEPS = WINDOWS[0] // DILATIONS[0]
N_KEYS = N_STEPS + 1
BLK = 128
CONV_K = 3
N_BUCKETS = 32
MAX_DISTANCE = WINDOWS[-1]
N_EXPERTS = 64
TOP_K = 8
N_ROUTE_GROUPS = 8
TOPK_GROUPS = 4
D_EXPERT = D_MODEL // 4
ROUTED_SCALE = 2.5
MOE_CHUNK = 512
RMS_EPS = 1e-6
N_PROJ = 3 * ATTN_WIDTH + 3 * CONV_CH

kernel_name = 'hymba_dilated_swa_shortconv_moe_step'

def _rmsnorm(x, g):
    xf = x.astype(jnp.float32)
    y = xf * lax.rsqrt(jnp.mean(xf * xf, axis=-1, keepdims=True) + RMS_EPS)
    return (y * g.astype(jnp.float32)).astype(x.dtype)

def _adaln(c, w_ada, b_ada):
    m = jax.nn.silu(c) @ w_ada + b_ada
    return jnp.split(m[:, None, :], 6, axis=-1)

def _t5_bucket(dist):
    max_exact = N_BUCKETS // 2
    df = jnp.maximum(dist, 1).astype(jnp.float32)
    large = max_exact + (jnp.log(df / max_exact) / math.log(MAX_DISTANCE / max_exact)
                         * (N_BUCKETS - max_exact)).astype(jnp.int32)
    large = jnp.minimum(large, N_BUCKETS - 1)
    return jnp.where(dist < max_exact, dist, large)

def _step_bias(rel_bias_g, dil):
    dist = jnp.arange(N_KEYS, dtype=jnp.int32) * dil
    return rel_bias_g[_t5_bucket(dist)].T.astype(jnp.float32)

def _dilated_attn_prompt(q, k, v, bias_k, dil):
    B_, S_, H, dh = q.shape
    L = S_ // dil
    Bd = B_ * dil

    def to_sub(a):
        return a.reshape(B_, L, dil, H, dh).transpose(0, 2, 1, 3, 4).reshape(Bd, L, H, dh)

    qs, ks, vs = to_sub(q), to_sub(k), to_sub(v)
    nb = -(-L // BLK)
    Lp = nb * BLK
    pad_end = Lp - L
    qb = jnp.pad(qs, ((0, 0), (0, pad_end), (0, 0), (0, 0))).reshape(Bd, nb, BLK, H, dh)

    def band(a):
        ap = jnp.pad(a, ((0, 0), (BLK, pad_end), (0, 0), (0, 0)))
        prev = ap[:, :Lp].reshape(Bd, nb, BLK, H, dh)
        cur = ap[:, BLK:].reshape(Bd, nb, BLK, H, dh)
        return jnp.concatenate([prev, cur], axis=2)

    kb, vb = band(ks), band(vs)
    s = jnp.einsum('znqhd,znkhd->znhqk', qb, kb,
                   preferred_element_type=jnp.float32) * (HEAD_DIM ** -0.5)
    qi = jnp.arange(BLK)[:, None]
    kj = jnp.arange(2 * BLK)[None, :]
    step = qi + BLK - kj
    key_sub = jnp.arange(nb)[:, None, None] * BLK - BLK + kj[None]
    valid = (step >= 0)[None] & (step <= N_STEPS)[None] & (key_sub >= 0)
    bias = bias_k[:, jnp.clip(step, 0, N_STEPS)]
    s = jnp.where(valid[None, :, None], s + bias[None, None], -jnp.inf)
    m = jnp.max(s, axis=-1, keepdims=True)
    p = jnp.exp(s - m)
    z = jnp.sum(p, axis=-1, keepdims=True)
    o = jnp.einsum('znhqk,znkhd->znqhd', (p / z).astype(vb.dtype), vb)
    lse = (m + jnp.log(z))[..., 0]
    o = o.reshape(Bd, Lp, H, dh)[:, :L]
    o = o.reshape(B_, dil, L, H, dh).transpose(0, 2, 1, 3, 4).reshape(B_, S_, H, dh)
    lse = lse.transpose(0, 1, 3, 2).reshape(Bd, Lp, H)[:, :L]
    lse = lse.reshape(B_, dil, L, H).transpose(0, 2, 1, 3).reshape(B_, S_, H)
    return o, lse

def _dilated_attn_sample(q, k_new, v_new, k_buf, v_buf, bias_k, dil):
    Wb = k_buf.shape[1]
    T = q.shape[1]
    k_ext = jnp.concatenate([k_buf.astype(k_new.dtype), k_new], axis=1)
    v_ext = jnp.concatenate([v_buf.astype(v_new.dtype), v_new], axis=1)
    idx = Wb + jnp.arange(T)[:, None] - jnp.arange(N_KEYS)[None, :] * dil
    valid = idx >= 0
    idx_c = jnp.maximum(idx, 0)
    kg = k_ext[:, idx_c]
    vg = v_ext[:, idx_c]
    s = jnp.einsum('bthd,btkhd->bhtk', q, kg,
                   preferred_element_type=jnp.float32) * (HEAD_DIM ** -0.5)
    s = jnp.where(valid[None, None], s + bias_k[:, None, :][None], -jnp.inf)
    m = jnp.max(s, axis=-1, keepdims=True)
    p = jnp.exp(s - m)
    z = jnp.sum(p, axis=-1, keepdims=True)
    o = jnp.einsum('bhtk,btkhd->bthd', (p / z).astype(vg.dtype), vg)
    lse = (m + jnp.log(z))[..., 0].transpose(0, 2, 1)
    return o, lse, k_ext[:, -Wb:], v_ext[:, -Wb:]

def _moe(h, w_router, b_router, w_gate_e, w_up_e, w_down_e, w_gate_s, w_up_s, w_down_s):
    B_, T_, D = h.shape
    xt = h.reshape(-1, D)
    n = xt.shape[0]
    scores = jax.nn.sigmoid((xt @ w_router).astype(jnp.float32))
    sel = scores + b_router.astype(jnp.float32)
    grp = sel.reshape(n, N_ROUTE_GROUPS, N_EXPERTS // N_ROUTE_GROUPS)
    grp_score = jnp.sum(lax.top_k(grp, 2)[0], axis=-1)
    _, gidx = lax.top_k(grp_score, TOPK_GROUPS)
    gmask = jnp.any(gidx[..., None] == jnp.arange(N_ROUTE_GROUPS), axis=1)
    emask = jnp.repeat(gmask, N_EXPERTS // N_ROUTE_GROUPS, axis=1)
    _, eidx = lax.top_k(jnp.where(emask, sel, -jnp.inf), TOP_K)
    w = jnp.take_along_axis(scores, eidx, axis=-1)
    w = w / jnp.sum(w, axis=-1, keepdims=True) * ROUTED_SCALE
    gates = jnp.sum(jax.nn.one_hot(eidx, N_EXPERTS, dtype=jnp.float32) * w[..., None], axis=1)
    gates = gates.astype(xt.dtype)
    chunk = min(MOE_CHUNK, n)
    pad = (-n) % chunk
    xp = jnp.pad(xt, ((0, pad), (0, 0))).reshape(-1, chunk, D)
    gp = jnp.pad(gates, ((0, pad), (0, 0))).reshape(-1, chunk, N_EXPERTS)

    def chunk_fn(args):
        xc, gc = args
        a = jnp.einsum('nd,edf->nef', xc, w_gate_e)
        b = jnp.einsum('nd,edf->nef', xc, w_up_e)
        hc = jax.nn.silu(a) * b * gc[..., None]
        return jnp.einsum('nef,efd->nd', hc, w_down_e)

    routed = lax.map(chunk_fn, (xp, gp)).reshape(-1, D)[:n]
    shared = (jax.nn.silu(xt @ w_gate_s) * (xt @ w_up_s)) @ w_down_s
    return (routed + shared).reshape(B_, T_, D)

def _trunk_layer(x, c, conv_prev, attend, rel_bias, norm1_g, norm2_g, w_ada, b_ada, w_in,
                 q_norm_g, k_norm_g, conv_w, w_o, w_router, b_router, w_gate_e, w_up_e,
                 w_down_e, w_gate_s, w_up_s, w_down_s):
    B_, T_, _ = x.shape
    sh1, sc1, g1, sh2, sc2, g2 = _adaln(c, w_ada, b_ada)
    h = _rmsnorm(x, norm1_g) * (1 + sc1) + sh1
    proj = h @ w_in
    A, C = ATTN_WIDTH, CONV_CH
    q, k, v, u_in, gate_b, gate_c = jnp.split(
        proj, [A, 2 * A, 3 * A, 3 * A + C, 3 * A + 2 * C], axis=-1)
    q = _rmsnorm(q.reshape(B_, T_, N_ATTN_HEADS, HEAD_DIM), q_norm_g)
    k = _rmsnorm(k.reshape(B_, T_, N_ATTN_HEADS, HEAD_DIM), k_norm_g)
    v = v.reshape(B_, T_, N_ATTN_HEADS, HEAD_DIM)
    outs, lses, states = [], [], []
    for g in range(N_DIL_GROUPS):
        hs = slice(g * HEADS_PER_GROUP, (g + 1) * HEADS_PER_GROUP)
        bias_k = _step_bias(rel_bias[:, hs], DILATIONS[g])
        o, lse, k_keep, v_keep = attend(g, q[:, :, hs], k[:, :, hs], v[:, :, hs], bias_k)
        outs.append(o)
        lses.append(lse)
        states += [k_keep, v_keep]
    wg = jax.nn.softmax(jnp.stack(lses, axis=0), axis=0)
    attn = jnp.concatenate(
        [(outs[g] * wg[g][..., None].astype(outs[g].dtype)).reshape(B_, T_, -1)
         for g in range(N_DIL_GROUPS)], axis=-1)
    u = gate_c * u_in
    up = jnp.concatenate([conv_prev.astype(u.dtype), u], axis=1)
    conv = sum(conv_w[j] * up[:, j:j + T_] for j in range(CONV_K))
    conv_out = gate_b * conv
    x = x + g1 * (jnp.concatenate([attn, conv_out], axis=-1) @ w_o)
    h2 = _rmsnorm(x, norm2_g) * (1 + sc2) + sh2
    x = x + g2 * _moe(h2, w_router, b_router, w_gate_e, w_up_e, w_down_e,
                      w_gate_s, w_up_s, w_down_s)
    states.append(up[:, -(CONV_K - 1):])
    return x, states

def setup_inputs(seed: int = 0) -> dict:
    key = jax.random.key(seed)
    ks = jax.random.split(key, 40)
    f32 = jnp.float32

    def nrm(k, shape, s):
        return jax.random.normal(k, shape, f32) * s

    wbs = [min(w, PAST_LEN) for w in WINDOWS]
    cshape = lambda wb: (DEPTH, DEC_BATCH, wb, HEADS_PER_GROUP, HEAD_DIM)
    return {
        'x_prompt': nrm(ks[0], (BATCH, SEQ, D_MODEL), 1.0),
        'x_sample': nrm(ks[1], (DEC_BATCH, DEC_SEQ, D_MODEL), 1.0),
        'c_prompt': nrm(ks[2], (BATCH, D_MODEL), 1.0),
        'c_sample': nrm(ks[3], (DEC_BATCH, D_MODEL), 1.0),
        'cache_k_w128': nrm(ks[4], cshape(wbs[0]), 1.0),
        'cache_v_w128': nrm(ks[5], cshape(wbs[0]), 1.0),
        'cache_k_w512': nrm(ks[6], cshape(wbs[1]), 1.0),
        'cache_v_w512': nrm(ks[7], cshape(wbs[1]), 1.0),
        'cache_k_w2048': nrm(ks[8], cshape(wbs[2]), 1.0),
        'cache_v_w2048': nrm(ks[9], cshape(wbs[2]), 1.0),
        'state_conv': nrm(ks[10], (DEPTH, DEC_BATCH, CONV_K - 1, CONV_CH), 1.0),
        'rel_bias': nrm(ks[11], (N_BUCKETS, N_ATTN_HEADS), 0.5),
        'norm1_g': 1.0 + nrm(ks[12], (DEPTH, D_MODEL), 0.01),
        'norm2_g': 1.0 + nrm(ks[13], (DEPTH, D_MODEL), 0.01),
        'w_ada': nrm(ks[14], (DEPTH, D_MODEL, 6 * D_MODEL), 0.5 * D_MODEL ** -0.5),
        'b_ada': nrm(ks[15], (DEPTH, 6 * D_MODEL), 0.02),
        'w_in': nrm(ks[16], (DEPTH, D_MODEL, N_PROJ), D_MODEL ** -0.5),
        'q_norm_g': 1.0 + nrm(ks[17], (DEPTH, HEAD_DIM), 0.01),
        'k_norm_g': 1.0 + nrm(ks[18], (DEPTH, HEAD_DIM), 0.01),
        'conv_w': nrm(ks[19], (DEPTH, CONV_K, CONV_CH), CONV_K ** -0.5),
        'w_o': nrm(ks[20], (DEPTH, ATTN_WIDTH + CONV_CH, D_MODEL), (ATTN_WIDTH + CONV_CH) ** -0.5),
        'w_router': nrm(ks[21], (DEPTH, D_MODEL, N_EXPERTS), D_MODEL ** -0.5),
        'b_router': nrm(ks[22], (DEPTH, N_EXPERTS), 0.01),
        'w_gate_e': nrm(ks[23], (DEPTH, N_EXPERTS, D_MODEL, D_EXPERT), D_MODEL ** -0.5),
        'w_up_e': nrm(ks[24], (DEPTH, N_EXPERTS, D_MODEL, D_EXPERT), D_MODEL ** -0.5),
        'w_down_e': nrm(ks[25], (DEPTH, N_EXPERTS, D_EXPERT, D_MODEL), D_EXPERT ** -0.5),
        'w_gate_s': nrm(ks[26], (DEPTH, D_MODEL, D_EXPERT), D_MODEL ** -0.5),
        'w_up_s': nrm(ks[27], (DEPTH, D_MODEL, D_EXPERT), D_MODEL ** -0.5),
        'w_down_s': nrm(ks[28], (DEPTH, D_EXPERT, D_MODEL), D_EXPERT ** -0.5),
    }

def reference(x_prompt, x_sample, c_prompt, c_sample, cache_k_w128, cache_v_w128,
              cache_k_w512, cache_v_w512, cache_k_w2048, cache_v_w2048, state_conv,
              rel_bias, norm1_g, norm2_g, w_ada, b_ada, w_in, q_norm_g, k_norm_g, conv_w,
              w_o, w_router, b_router, w_gate_e, w_up_e, w_down_e, w_gate_s, w_up_s,
              w_down_s):
    layer_w = (norm1_g, norm2_g, w_ada, b_ada, w_in, q_norm_g, k_norm_g, conv_w, w_o,
               w_router, b_router, w_gate_e, w_up_e, w_down_e, w_gate_s, w_up_s, w_down_s)
    caches_k = (cache_k_w128, cache_k_w512, cache_k_w2048)
    caches_v = (cache_v_w128, cache_v_w512, cache_v_w2048)

    def prompt_attend(g, q, k, v, bias_k):
        o, lse = _dilated_attn_prompt(q, k, v, bias_k, DILATIONS[g])
        keep = min(WINDOWS[g], k.shape[1])
        return o, lse, k[:, -keep:], v[:, -keep:]

    yp = x_prompt
    states_p = []
    for l in range(DEPTH):
        conv0 = jnp.zeros((yp.shape[0], CONV_K - 1, CONV_CH), yp.dtype)
        yp, st = _trunk_layer(yp, c_prompt, conv0, prompt_attend, rel_bias,
                              *[w[l] for w in layer_w])
        states_p.append(st)

    ys = x_sample
    states_s = []
    for l in range(DEPTH):
        def sample_attend(g, q, k, v, bias_k, l=l):
            return _dilated_attn_sample(q, k, v, caches_k[g][l], caches_v[g][l],
                                        bias_k, DILATIONS[g])
        ys, st = _trunk_layer(ys, c_sample, state_conv[l], sample_attend, rel_bias,
                              *[w[l] for w in layer_w])
        states_s.append(st)

    sp = [jnp.stack([states_p[l][i] for l in range(DEPTH)]) for i in range(7)]
    ss = [jnp.stack([states_s[l][i] for l in range(DEPTH)]) for i in range(7)]
    k128_p, v128_p, k512_p, v512_p, k2048_p, v2048_p, conv_p = sp
    k128_s, v128_s, k512_s, v512_s, k2048_s, v2048_s, conv_s = ss
    return (yp, ys, k128_p, v128_p, k512_p, v512_p, k2048_p, v2048_p, conv_p,
            k128_s, v128_s, k512_s, v512_s, k2048_s, v2048_s, conv_s)


_drawn_inputs = setup_inputs


def setup_inputs(seed=0):
    import zlib

    import numpy as np

    out = dict(_drawn_inputs(seed))
    spreads = {}
    factors = {}
    for name, (base, spread) in spreads.items():
        noise = np.random.default_rng([zlib.crc32(name.encode()), seed]).standard_normal(out[name].shape)
        drawn = base * np.exp(spread * noise) if base else spread * noise
        out[name] = __import__('jax').numpy.asarray(drawn.astype(out[name].dtype))
    for name, factor in factors.items():
        out[name] = (out[name] * factor).astype(out[name].dtype)
    return out
```

```python
from contextlib import ExitStack

import numpy as np
import concourse.bass as bass
from concourse import mybir

F32 = mybir.dt.float32
BF16 = mybir.dt.bfloat16
I32 = mybir.dt.int32
ALU = mybir.AluOpType
ACT = mybir.ActivationFunctionType
AX = mybir.AxisListType.X

P = 128
D = 1024
KD = D // P
SEQ = 512
DIL = 4
PT_ = SEQ // DIL
B = 8
T = 4
NS = B * T
NTOK = SEQ + NS
TILES = 5
SAMPLE = 4
ORDER = [4, 0, 1, 2, 3]
G = 3
H = 4
DH = 64
GW = H * DH
AW = G * GW
CC = 256
NE = 64
FE = 256
NPROJ = 3 * AW + 3 * CC
WB = (128, 512, 1024)
DILS = (1, 4, 16)
STEPS = 128
NEG = -1.0e30
EPS = 1e-6
SEC = 6 * D
ADA_W = 256
ADA_N = SEC // ADA_W
ADA_1 = 2 * D // ADA_W
PJ_W = 384
WO_W = (384, 384, 256)
RING = 3
KB = 3
VB = 7
SLOT = KD * PJ_W
NVEC = 9
VL = 2 * P
KEYS = (128, 128, 64)
SEG = tuple(k + NS for k in KEYS)
SOFF = (0, SEG[0], SEG[0] + SEG[1])
SW = sum(SEG)
HROW = D + NE
TR = NTOK + P
ET = 2
MAXT = NE + NTOK * 8 // P + ET


def bucket(dist):
    if dist < 16:
        return dist
    large = 16 + int(np.float32(np.log(np.float32(dist) / np.float32(16))) / np.float32(np.log(2048 / 16))
                     * np.float32(16))
    return min(large, 31)


CST = {}
_off = 0
for _name, _w in (("ident", P), ("flip", P), ("iota", P), ("upper", P), ("ones", P), ("smask", SW), ("negt", P), ("slot", 16),
                  ("tri8", 64), ("dummy", 1), ("negdummy", 1), ("iotacol", 1), ("each", P + NS)):
    CST[_name] = (_off, _w)
    _off += _w
CSTW = _off


def constants():
    c = np.zeros((P, CSTW), np.float32)

    def put(name, a):
        o, w = CST[name]
        c[:, o:o + w] = a
    i = np.arange(P)
    put("ident", np.eye(P))
    put("flip", np.eye(P)[::-1])
    put("iota", np.broadcast_to(i, (P, P)))
    put("upper", i[:, None] < i[None, :])
    put("ones", 1.0)
    m = np.full((P, SW), NEG, np.float32)
    for p in range(P):
        b, t = (p % NS) // T, p % T
        for g in range(G):
            for l in range(KEYS[g]):
                if g > 0 or l >= t:
                    m[p, SOFF[g] + l] = 0.0
            for n in range(T):
                if (n <= t) if g == 0 else (n == t):
                    m[p, SOFF[g] + KEYS[g] + b * T + n] = 0.0
    put("smask", m)
    put("negt", np.broadcast_to(-P * i, (P, P)))
    s = np.zeros((P, 16), np.float32)
    for k in range(TILES):
        s[:, 3 * k] = P * k
        s[:, 3 * k + 1] = i
        s[:, 3 * k + 2] = 1.0
    put("slot", s)
    put("tri8", np.broadcast_to((np.arange(8)[None, :] < np.arange(8)[:, None]).reshape(-1), (P, 64)))
    put("dummy", (NTOK + i)[:, None])
    put("negdummy", -(NTOK + i)[:, None])
    put("iotacol", i[:, None])
    e = np.zeros((P, P + NS), np.float32)
    e[0, 0:P] = 1.0
    for b in range(B):
        e[1 + b, P + T * b:P + T * (b + 1)] = 1.0
    put("each", e)
    ohp = np.zeros((33, NVEC, VL), np.float32)
    for v in range(NVEC):
        for y in range(VL):
            x = 127 - y
            if v < 7:
                d = 4 * x + 3 - v
                step, dist = d, d
                ok = 0 <= d <= STEPS
            elif v == 7:
                dist, ok = 4 * x, x >= 0
            else:
                dist, ok = 4 * x, x >= 0 and x % 4 == 0
            if ok:
                ohp[bucket(dist), v, y] = 1.0
            else:
                ohp[32, v, y] = NEG
    ohs = np.zeros((32, T, SW), np.float32)
    for t in range(T):
        for g in range(G):
            for l in range(KEYS[g]):
                j = (STEPS + t - l) if g == 0 else (KEYS[g] - l)
                if 0 <= j <= STEPS:
                    ohs[bucket(j * DILS[g]), t, SOFF[g] + l] = 1.0
            for n in range(NS):
                j = (t - n % T) if g == 0 else 0
                if j >= 0:
                    ohs[bucket(j), t, SOFF[g] + KEYS[g] + n] = 1.0
    sel = np.zeros((G * H, G, T, P), np.float32)
    for g in range(G):
        for h in range(H):
            for p in range(P):
                if p // NS == h:
                    sel[g * H + h, g, p % T, p] = 1.0
    return {"k_cst": c, "k_ohp": ohp.reshape(33, -1), "k_ohs": ohs.reshape(32, -1), "k_sel": sel.reshape(G * H, -1)}


KSEG = (((0, 0, 256), (1, 256, 384)), ((1, 0, 128), (2, 128, 384)))


def row_writes():
    out, total, sample_q = [], [0, 0, 0], 0
    for z in range(20):
        sample = ORDER[z % 5] == SAMPLE
        if z < 10:
            sample_q += 16 * sample
            out.append(("q", sample_q) if sample else (None, 0))
        else:
            total[z % 3] += 16 if sample else 32
            out.append((z % 3, total[z % 3]))
    return out, total


KN_OUT, KOUT = row_writes()
YB = (0, 1, 4, 5)


def ring_items():
    items = [("ada", i) for i in range(ADA_1)]
    for c in range(NPROJ // PJ_W):
        items += [("proj", c), ("ada", ADA_1 + 2 * c), ("ada", ADA_1 + 2 * c + 1)]
    items += [("wo", 0), ("wo", 1), ("wo", 2), ("sgate", 0), ("sup", 0), ("sdown", 0)]
    return items


def build(nc, a, out):
    (y_p, y_s, kp0, vp0, kp1, vp1, kp2, vp2, conv_p, ks0, vs0, ks1, vs1, ks2, vs2, conv_s) = out
    k_prompt, v_prompt, k_sample, v_sample = (kp0, kp1, kp2), (vp0, vp1, vp2), (ks0, ks1, ks2), (vs0, vs1, vs2)
    k_cache = (a["cache_k_w128"], a["cache_k_w512"], a["cache_k_w2048"])
    v_cache = (a["cache_v_w128"], a["cache_v_w512"], a["cache_v_w2048"])
    mods_d = nc.dram_tensor("mods_d", [1 + B, SEC], F32, kind="Internal").ap()
    new_d = nc.dram_tensor("new_d", [3, NS, AW], F32, kind="Internal").ap()
    bias_d = nc.dram_tensor("bias_d", [G * H, NVEC * VL], F32, kind="Internal").ap()
    h2_d = nc.dram_tensor("h2_d", [TR, HROW], F32, kind="Internal").ap()
    y_d = nc.dram_tensor("y_d", [TR, D], F32, kind="Internal").ap()

    w_ada = a["w_ada"].rearrange("z (k p) n -> p (z k) n", p=P)
    w_in = a["w_in"].rearrange("z (k p) n -> p (z k) n", p=P)
    w_o = a["w_o"].rearrange("z (k p) n -> p (z k) n", p=P)
    xp = a["x_prompt"].rearrange("z (l r) d -> (z r) l d", r=DIL)
    xs = a["x_sample"].rearrange("b t d -> (b t) d")
    yp = y_p.rearrange("z (l r) d -> (z r) l d", r=DIL)
    ys = y_s.rearrange("b t d -> (b t) d")

    with ExitStack() as ctx:
        mem = ctx.enter_context(nc.sbuf_tensor("mem", [P, 53100], F32))
        top = [0]

        def take(n):
            top[0] += n
            assert top[0] <= 53100, top[0]
            return top[0] - n

        def at(off, *dims, parts=P):
            n = int(np.prod(dims))
            v = mem[0:parts, off:off + n]
            if len(dims) == 2:
                v = v.rearrange("p (a b) -> p a b", a=dims[0])
            elif len(dims) == 3:
                v = v.rearrange("p (a b c) -> p a b c", a=dims[0], b=dims[1])
            return v

        def tensor(*dims, parts=P):
            return at(take(int(np.prod(dims))), *dims, parts=parts)

        def sem(name):
            return ctx.enter_context(nc.semaphore(name))

        m_ring = take(RING * SLOT)
        m_hT = take(KD * NTOK)
        m_qk = take(2 * 6 * NTOK)
        m_vr = take(TILES * AW)
        m_kn = take(5 * PJ_W)
        m_mod = take(4 * D)
        m_smp = take(7 * D)
        m_att = take(3072)
        m_cv = take(3204)
        ring = [at(m_ring + SLOT * i, SLOT) for i in range(RING)]
        x_t = tensor(TILES, D)
        hT = at(m_hT, KD, NTOK)
        catT = at(m_hT, KD, NTOK)
        qT, kT = at(m_qk, 6, NTOK), at(m_qk + 6 * NTOK, 6, NTOK)
        h2T = at(m_qk, KD, NTOK)
        hs = at(m_qk + KD * NTOK, 2, NTOK)
        v_r = at(m_vr, TILES, AW)
        kn = [at(m_kn + PJ_W * i, PJ_W) for i in range(3)]
        sq = [at(m_kn + PJ_W * (3 + i), PJ_W) for i in range(2)]
        wt = [at(m_kn + PJ_W * i, PJ_W) for i in range(2)]
        m1 = [[at(m_mod + D * (2 * s + i), D) for i in range(2)] for s in range(2)]
        tb = [at(m_mod + NVEC * P * i, NVEC, P) for i in range(2)]
        ohp, ohs = at(m_smp, NVEC * VL, parts=33), at(m_smp + NVEC * VL, T * SW, parts=32)
        sel = at(m_smp + NVEC * VL + T * SW, G, T, P, parts=G * H)
        k_buf = [at(m_smp + D * i, D) for i in range(KB)]
        q_buf = [at(m_smp + D * (KB + i), D) for i in range(KB)]
        prod = at(m_smp + D * 2 * KB, D)
        v_buf = [at(m_smp + D * i, D) for i in range(VB)]
        m2 = [[at(m_smp + D * (3 * s + i), D) for i in range(3)] for s in range(2)]
        h_row = [at(m_att + D * i, D) for i in range(2)]
        junk = at(m_att + 2 * D, D)
        crow = at(m_att, D, parts=1 + B)
        csig = at(m_att + D, D, parts=1 + B)
        sc_t = [at(m_att + 768 * i, 768) for i in range(2)]
        pT_t = [at(m_att + 768 * (2 + i), 768) for i in range(2)]
        bv = at(m_qk, NVEC * VL, parts=G * H)
        bs = at(m_cv, T * SW, parts=G * H)
        upP = at(m_cv, 2, 2 + SEQ)
        uT = at(m_cv + 2 * (2 + SEQ), 2, NTOK)
        gT = at(m_cv + 2 * (2 + SEQ) + 2 * NTOK, 2, NTOK)
        cst = tensor(CSTW)

        def const(name, parts=P, w=None):
            o, width = CST[name]
            return cst[0:parts, o:o + (w or width)]
        cT = tensor(KD * (1 + B))
        mrow = tensor(4, ADA_W, parts=1 + B)
        relb = tensor(G * H, parts=33)
        gq = tensor(DH)
        gk = tensor(DH)
        rows19 = at(m_vr + P, CC, parts=19)
        t19 = tensor(2, 19)
        upS = tensor(2, B, 2 + T)
        csx = tensor(2, 18)
        cso = at(m_att + 2 * D, CC, parts=18)
        st = tensor(G, P)
        stn = at(m_kn + 4 * PJ_W, G, P, parts=NS)
        ts = tensor(SW)
        sp = tensor(SW)
        spT = at(m_kn + 2 * PJ_W, 2 * G, P)
        wr = at(m_smp + 6 * D, KD, NE)
        br = tensor(NE)
        small = tensor(96)
        ss1, rs1, ss2, rs2 = (small[:, 8 * i:8 * i + TILES] for i in range(4))
        ssq = [small[:, 32 + 8 * i:38 + 8 * i] for i in range(2)]
        nmx, zs, rz = (small[:, 48 + 4 * i:50 + 4 * i] for i in range(3))
        snm, szs, srz = (small[:, 60 + i:61 + i] for i in range(3))

        h2_row = h_row
        sg = at(m_cv, 2, NTOK)
        y_row = [at(m_cv + 2 * NTOK + D * i, D) for i in range(2)]
        RW = TILES * NE
        r_sc, r_sel, r_ma, r_mr, r_m, r_g, r_pos, r_t8, r_gt, r_eq = (at(m_vr + RW * i, RW) for i in range(10))
        m_r = m_vr + 10 * RW
        r_gs, r_rank, r_gmb = (at(m_r + 40 * i, 40) for i in range(3))
        r_den = at(m_r + 120, TILES)
        r_cnt, r_nt, r_incl, r_base, r_cmp = (at(m_r + 128 + NE * i, NE) for i in range(5))
        r_top = at(m_r + 128 + 5 * NE, TILES, 8)
        zero = at(m_mod, HROW)
        g2 = [at(m_kn, D), at(m_att + 2 * D, D)]
        xg = [at(m_mod + HROW * i, HROW) for i in range(ET)]
        xT = [at(m_att + D * i, KD, P) for i in range(ET)]
        yo = [at(m_cv + D * i, D) for i in range(ET)]
        sge = [at(m_cv + 2 * D + FE * i, 2, P) for i in range(ET)]
        he = [at(m_cv + 2 * D + 2 * FE + FE * i, 2, P) for i in range(ET)]
        oneh = [at(m_kn + D + RW * i, RW).bitcast(BF16).rearrange("p (k n) -> p k n", k=TILES) for i in range(ET)]
        m_gu, m_dn = (m_hT, m_smp), (m_ring, m_smp + 4 * D)
        wgu = [at(m, 2, KD, FE) for m in m_gu]
        wdn = [at(m, 2, D) for m in m_dn]
        yf = [at(m_ring + D * i, D) for i in range(TILES)]
        meta = tensor(P + 8, parts=1).bitcast(I32)
        ecol = tensor(1)
        fcnt = tensor(1, parts=1)
        fpair = r_t8[0:1, 0:P]
        slotb = tensor(8).bitcast(BF16)
        ix = [tensor(1).bitcast(I32) for _ in range(ET)]
        ixs = [tensor(1).bitcast(I32) for _ in range(ET)]
        imt = tensor(3)
        gcol = [tensor(1) for _ in range(ET)]

        pb = [ctx.enter_context(nc.psum_tensor(f"pb{i}", [P, 512], F32)) for i in range(8)]

        s_cst, s_oh, s_in, s_x = sem("s_cst"), sem("s_oh"), sem("s_in"), sem("s_x")
        s_ring = [sem(f"s_ring{i}") for i in range(RING)]
        s_ones, s_csig, s_cs, s_small = sem("s_ones"), sem("s_csig"), sem("s_cs"), sem("s_small")
        s_cT, s_smallT = sem("s_cT"), sem("s_smallT")
        s_bmm, s_bev, s_bvw, s_tsmm, s_ts = sem("s_bmm"), sem("s_bev"), sem("s_bvw"), sem("s_tsmm"), sem("s_ts")
        s_ada, s_mrow, s_each = sem("s_ada"), sem("s_mrow"), sem("s_each")
        s_modw = [sem(f"s_modw{i}") for i in range(4)]
        s_m1, s_m2, s_wr = sem("s_m1"), sem("s_m2"), sem("s_wr")
        s_ss1, s_var1, s_sd1, s_rs1 = sem("s_ss1"), sem("s_var1"), sem("s_sd1"), sem("s_rs1")
        s_h, s_hTp, s_hT = sem("s_h"), sem("s_hTp"), sem("s_hT")
        s_pj, s_sq, s_var, s_sd, s_pjq, s_kn, s_pjv, s_cmul = (sem(n) for n in (
            "s_pj", "s_sq", "s_var", "s_sd", "s_pjq", "s_kn", "s_pjv", "s_cmul"))
        s_qkp, s_qk = sem("s_qkp"), sem("s_qk")
        s_kout = [sem(f"s_kout{i}") for i in range(3)]
        s_qout, s_vout, s_cout = sem("s_qout"), sem("s_vout"), sem("s_cout")
        s_link = sem("s_link")
        s_kq = [sem(f"s_kq{i}") for i in range(KB)]
        s_vb = [sem(f"s_vb{i}") for i in range(VB)]
        s_sco, s_snew, s_snT, s_sS, s_smx, s_sex, s_sP, s_sPTp, s_sPT, s_spv, s_sO = (sem(n) for n in (
            "s_sco", "s_snew", "s_snT", "s_sS", "s_smx", "s_sex", "s_sP", "s_sPTp", "s_sPT", "s_spv", "s_sO"))
        s_csx, s_csT, s_cso, s_conv = sem("s_csx"), sem("s_csT"), sem("s_cso"), sem("s_conv")
        s_tb = [sem(f"s_tb{i}") for i in range(2)]
        s_S, s_add, s_mx, s_ex, s_P, s_Tp, s_T, s_O, s_Oe = (sem(n) for n in (
            "s_S", "s_add", "s_mx", "s_ex", "s_P", "s_Tp", "s_T", "s_O", "s_Oe"))
        s_wo, s_wg, s_x1 = sem("s_wo"), sem("s_wg"), sem("s_x1")
        s_caches, s_newrows = sem("s_caches"), sem("s_newrows")

        s_ss2, s_var2, s_sd2, s_h2, s_h2p, s_h2T = (sem(n) for n in (
            "s_ss2", "s_var2", "s_sd2", "s_h2", "s_h2p", "s_h2T"))
        s_h2w = [sem(f"s_h2w{i}") for i in range(2)]
        s_yw = [sem(f"s_yw{i}") for i in range(2)]
        s_lg, s_rz, s_sc, s_su, s_sg, s_hs, s_sd_, s_ysh, s_M, s_G, s_gw, s_rank, s_ecol, s_eT, s_meta = (
            sem(n) for n in ("s_lg", "s_rz", "s_sc", "s_su", "s_sg", "s_hs", "s_sd_", "s_ysh", "s_M", "s_G", "s_gw",
                             "s_rank", "s_ecol", "s_eT", "s_meta"))
        s_zero, s_zw, s_g2 = sem("s_zero"), sem("s_zw"), sem("s_g2")
        s_oneh, s_im, s_ix, s_tp, s_xa, s_xd, s_gc, s_upg, s_up, s_si, s_he, s_dn, s_ya, s_yd, s_ixs, s_sca = (
            sem(n) for n in ("s_oneh", "s_im", "s_ix", "s_tp", "s_xa", "s_xd", "s_gc", "s_upg", "s_up", "s_si", "s_he",
                             "s_dn", "s_ya", "s_yd", "s_ixs", "s_sca"))
        s_ga = [sem(f"s_ga{i}") for i in range(ET)]
        s_wgu = [sem(f"s_wgu{i}") for i in range(ET)]
        s_wdn = [sem(f"s_wdn{i}") for i in range(ET)]
        s_lrow, s_all, s_yf, s_fin, s_yout = sem("s_lrow"), sem("s_all"), [sem(f"s_yf{i}") for i in range(TILES)], sem("s_fin"), sem("s_yout")

        block = ctx.enter_context(nc.Block())
        items = ring_items()

        def scale_of(i):
            return {1: "norm1_g", 4: "norm2_g"}.get(ADA_W * i // D)

        landed = []
        for n, (kind, i) in enumerate(items):
            dmas = 1 if kind != "ada" else 3 if scale_of(i) else 2
            landed.append((landed[n - RING] if n >= RING else 0) + 16 * dmas)

        def ada_row(n, q):
            return ring[n % RING][0:1 + B, KD * ADA_W + ADA_W * q:KD * ADA_W + ADA_W * (q + 1)]

        copies = []
        for caches, dsts in ((k_cache, k_sample), (v_cache, v_sample)):
            for g in range(G):
                per = (B, 2, 1)[g]
                for b in range(0, B, per):
                    copies.append((dsts[g][0, b:b + per].rearrange("b w h d -> b (w h d)")[:, 0:(WB[g] - T) * GW],
                                   caches[g][0, b:b + per].rearrange("b w h d -> b (w h d)")[:, T * GW:]))

        def ring_uses(kind, i):
            return items.index((kind, i))

        def tok(j):
            return slice(P * j, P * j + (NS if j == SAMPLE else P))

        def nt(j):
            return NS if j == SAMPLE else P

        def sc_row(n):
            return n // B, n % B

        def evac_count(z):
            return (s_pjq, z + 1) if z < 20 else (s_pjv, z - 19) if z < 34 else (s_cmul, z - 33)

        @block.sync
        def _(eng):
            eng.dma_start(cst[:], a["k_cst"]).then_inc(s_cst, 16)
            eng.dma_start(crow[0:1, :], a["c_prompt"]).then_inc(s_in, 16)
            eng.dma_start(crow[1:1 + B, :], a["c_sample"]).then_inc(s_in, 16)
            eng.dma_start(rows19[0:16, :], a["state_conv"].rearrange("z b j c -> (z b j) c")).then_inc(s_in, 16)
            eng.dma_start(rows19[16:19, :], a["conv_w"].rearrange("z j c -> (z j) c")).then_inc(s_in, 16)
            for n, (kind, i) in enumerate(items):
                if n >= RING:
                    k0, i0 = items[n - RING]
                    if k0 == "ada":
                        eng.wait_ge(s_mrow, i0 + 1)
                    elif k0 == "proj":
                        eng.wait_ge(s_pj, 5 * (i0 + 1) if i0 < 6 else 30 + 3 * (i0 - 5))
                    else:
                        eng.wait_ge(s_wo, 5 * (i0 + 1))
                slot = ring[n % RING]
                if kind == "ada":
                    dst = slot[:, 0:KD * ADA_W].rearrange("p (k n) -> p k n", k=KD)
                    src = w_ada[:, :, ADA_W * i:ADA_W * (i + 1)]
                    cols = [a["b_ada"][:, ADA_W * i:ADA_W * (i + 1)]]
                    if scale_of(i):
                        c0 = ADA_W * i % D
                        cols.append(a[scale_of(i)][:, c0:c0 + ADA_W])
                    for q, col in enumerate(cols):
                        eng.dma_start(ada_row(n, q), col.to_broadcast([1 + B, ADA_W])).then_inc(s_ring[n % RING], 16)
                elif kind == "proj":
                    dst = slot.rearrange("p (k n) -> p k n", k=KD)
                    src = w_in[:, :, PJ_W * i:PJ_W * (i + 1)]
                elif kind == "wo":
                    dst = slot[:, 0:KD * WO_W[i]].rearrange("p (k n) -> p k n", k=KD)
                    src = w_o[:, :, sum(WO_W[:i]):sum(WO_W[:i + 1])]
                elif kind == "sdown":
                    dst = slot[:, 0:2 * D].rearrange("p (k n) -> p k n", k=2)
                    src = a["w_down_s"].rearrange("z (k p) n -> p (z k) n", p=P)
                else:
                    dst = slot[:, 0:KD * FE].rearrange("p (k n) -> p k n", k=KD)
                    src = a["w_gate_s" if kind == "sgate" else "w_up_s"].rearrange("z (k p) n -> p (z k) n", p=P)
                eng.dma_start(dst, src).then_inc(s_ring[n % RING], 16)
                if n == RING:
                    for r in range(DIL):
                        eng.dma_start(x_t[:, r, :], xp[r]).then_inc(s_x, 16)
                    eng.dma_start(x_t[0:NS, SAMPLE, :], xs).then_inc(s_x, 16)
            eng.wait_ge(s_pjv, 10)
            for r in range(DIL):
                for g in range(G):
                    skip = max(0, SEQ - WB[g]) // DIL
                    dst = v_prompt[g].rearrange("z y (l r) h d -> (z y r) l (h d)", r=DIL)[r]
                    eng.dma_start(dst, v_r[skip:P, r, GW * g:GW * (g + 1)]).then_inc(s_vout, 16)
            eng.dma_start(new_d[2], v_r[0:NS, SAMPLE, :]).then_inc(s_vout, 16)
            for i in range(3):
                eng.wait_ge(s_kout[i], KOUT[i])
            eng.wait_ge(s_vout, 16 * (DIL * G + 1))
            for kv, dsts in ((1, k_sample), (2, v_sample)):
                for g in range(G):
                    eng.dma_start(dsts[g][0, :, WB[g] - T:, :, :].rearrange("b t h d -> b t (h d)"),
                                  new_d[kv].rearrange("(b t) n -> b t n", t=T)[:, :, GW * g:GW * (g + 1)]
                                  ).then_inc(s_newrows, 16)
            for j, tt in enumerate(ORDER):
                eng.wait_ge(s_h2, j + 1)
                eng.dma_start(h2_d[tok(tt), 0:D], h2_row[j % 2][0:nt(tt), :]).then_inc(s_h2w[j % 2], 16)
            eng.wait_ge(s_G, 1)
            for tt in range(TILES):
                eng.dma_start(h2_d[tok(tt), D:HROW], r_g[0:nt(tt), NE * tt:NE * (tt + 1)]).then_inc(s_gw, 16)
            eng.wait_ge(s_meta, 1)
            groups = eng.value_load(meta[0:1, P:P + 1], min_val=1, max_val=P // ET - 1)

            def weights(s, e, i):
                eng.wait_ge(s_up, ET * i + s + 1)
                for q, name in ((0, "w_gate_e"), (1, "w_up_e")):
                    eng.dma_start(wgu[s][:, q], a[name][0, bass.ds(e, 1)].rearrange("e (k p) f -> p (e k) f", p=P)
                                  ).then_inc(s_wgu[s], 16)
                eng.wait_ge(s_dn, 2 * (ET * i + s + 1))
                eng.dma_start(wdn[s], a["w_down_e"][0, bass.ds(e, 1)].rearrange("e (k p) n -> p (e k) n", p=P)
                              ).then_inc(s_wdn[s], 16)
            eng.wait_ge(s_su, 4)
            for s in range(ET):
                if s:
                    eng.wait_ge(s_ysh, 2 * TILES - 2)
                weights(s, eng.value_load(meta[0:1, s:s + 1], min_val=0, max_val=NE - 1), 0)
            with eng.Fori(1, groups) as i:
                for s in range(ET):
                    weights(s, eng.value_load(meta[0:1, bass.ds(ET * i + s, 1)], min_val=0, max_val=NE - 1), i)
            for s in range(ET):
                eng.wait_ge(s_wdn[s], 16 * groups)
            eng.wait_ge(s_all, 1)
            for tt in ORDER:
                eng.dma_start(yf[tt][0:nt(tt), :], y_d[tok(tt), :]).then_inc(s_yf[tt], 16)
            for s in range(ET):
                eng.wait_ge(s_wgu[s], 32 * groups)
            for j, tt in enumerate(ORDER):
                eng.wait_ge(s_fin, j + 1)
                eng.dma_start(ys if tt == SAMPLE else yp[tt], yf[tt][0:nt(tt), :]).then_inc(s_yout, 16)
            eng.wait_ge(s_caches, 16 * len(copies))
            eng.wait_ge(s_newrows, 16 * 6)
            eng.wait_ge(s_yout, 16 * TILES)

        @block.gpsimd
        def _(eng):
            eng.memset(relb[:], 1.0).then_inc(s_ones, 1)
            eng.dma_start(ohp[:], a["k_ohp"]).then_inc(s_oh, 16)
            eng.dma_start(ohs[:], a["k_ohs"]).then_inc(s_oh, 16)
            eng.dma_start(sel[:], a["k_sel"].rearrange("q (g t p) -> q g t p", g=G, t=T)).then_inc(s_oh, 16)
            eng.wait_ge(s_ones, 1)
            eng.dma_start(relb[0:32, :], a["rel_bias"]).then_inc(s_oh, 16)
            eng.dma_start(gq[:], a["q_norm_g"].to_broadcast([P, DH])).then_inc(s_small, 16)
            eng.dma_start(gk[:], a["k_norm_g"].to_broadcast([P, DH])).then_inc(s_small, 16)
            eng.dma_start(br[:], a["b_router"].to_broadcast([P, NE])).then_inc(s_small, 16)
            eng.wait_ge(s_bev, 5)
            eng.dma_start(bias_d, bv[:]).then_inc(s_bvw, 16)

            def mod_out(i):
                eng.wait_ge(s_mrow, i + 1)
                eng.dma_start(mods_d[:, ADA_W * i:ADA_W * (i + 1)], mrow[:, i % 4, :]).then_inc(s_modw[i % 4], 16)

            def bcast(dst, sec, sample):
                src = mods_d[1:1 + B, D * sec:D * (sec + 1)] if sample else mods_d[0:1, D * sec:D * (sec + 1)]
                if sample:
                    for t in range(T):
                        yield dst[t:NS:T, :], src
                else:
                    yield dst, src.to_broadcast([P, D])

            eng.wait_ge(s_ts, 1)
            for i in range(ADA_1, ADA_1 + 4):
                mod_out(i)
            eng.wait_ge(s_qout, 32)
            for n in range(G * B):
                g, b = sc_row(n)
                if n >= KB:
                    eng.wait_ge(s_sco, n - KB + 1)
                w = KEYS[g]
                rows = k_cache[g][0, b].rearrange("(l r) h d -> l (r h d)", r=DILS[g])
                eng.dma_start(k_buf[n % KB][0:w, 0:(GW if g == 0 else D)], rows[0:w, 0:(GW if g == 0 else D)]
                              ).then_inc(s_kq[n % KB], 16)
                qsrc = new_d[0, T * b:T * (b + 1), GW * g:GW * (g + 1)].unsqueeze(0).to_broadcast([w, T, GW])
                eng.dma_start(q_buf[n % KB][0:w, :].rearrange("p (t n) -> p t n", t=T), qsrc).then_inc(s_kq[n % KB], 16)
                if n % 5 == 2 and n > 2:
                    mod_out(ADA_1 + 4 + 2 * (n // 5 - 1))
                    mod_out(ADA_1 + 5 + 2 * (n // 5 - 1))
            for i in range(ADA_N - 4, ADA_N):
                mod_out(i)
            eng.wait_ge(s_bvw, 16)
            eng.wait_ge(s_h, TILES)

            def bias_table(h):
                for g, v0, nv in ((0, 0, 7), (1, 7, 1), (2, 8, 1)):
                    src = bass.AP(tensor=bias_d.tensor, offset=((g * H + h) * NVEC + v0) * VL,
                                  ap=[[1, P], [VL, nv], [1, P]])
                    eng.dma_start(tb[h % 2][:, v0:v0 + nv, :], src).then_inc(s_tb[h % 2], 16)
            bias_table(0)
            bias_table(1)

            def values(n):
                g, b = sc_row(n)
                if n >= VB:
                    eng.wait_ge(s_spv, n - VB + 1)
                w = KEYS[g]
                rows = v_cache[g][0, b].rearrange("(l r) h d -> l (r h d)", r=DILS[g])
                eng.dma_start(v_buf[n % VB][0:w, 0:(GW if g == 0 else D)], rows[0:w, 0:(GW if g == 0 else D)]
                              ).then_inc(s_vb[n % VB], 16)
            eng.wait_ge(s_sco, G * B)
            for n in range(VB):
                values(n)
            eng.wait_ge(s_add, H)
            bias_table(2)
            for n in range(VB, 2 * VB):
                values(n)
            eng.wait_ge(s_add, 2 * H)
            bias_table(3)
            for n in range(2 * VB, G * B):
                values(n)
            eng.wait_ge(s_spv, G * B)
            for i in range(4):
                eng.wait_ge(s_modw[i], 16 * ((ADA_N - ADA_1) // 4))
            for s in (1, 0):
                for i, sec in ((0, 2), (1, 4), (2, 3)):
                    for dst, src in bcast(m2[s][i], sec, s == 1):
                        eng.dma_start(dst, src).then_inc(s_m2, 16)
            eng.dma_start(wr[:], a["w_router"].rearrange("z (k p) e -> p (z k) e", p=P)).then_inc(s_wr, 16)
            eng.wait_ge(s_add, 16)
            eng.memset(zero[:], 0.0).then_inc(s_zero, 1)
            eng.wait_ge(s_zero, 1)
            eng.dma_start(h2_d[NTOK:TR, :], zero[:]).then_inc(s_zw, 16)
            eng.dma_start(y_d[NTOK:TR, :], zero[:, 0:D]).then_inc(s_sca, 16)
            eng.wait_ge(s_x1, 15)
            eng.wait_ge(s_ss2, TILES)
            for s in range(2):
                for dst, src in bcast(g2[s], 5, s == 1):
                    eng.dma_start(dst, src).then_inc(s_g2, 16)
            eng.wait_ge(s_zw, 16)
            for i in range(2):
                eng.wait_ge(s_h2w[i], 16 * (3 - i))
            eng.wait_ge(s_gw, 16 * TILES)
            eng.wait_ge(s_meta, 1)
            groups = eng.value_load(meta[0:1, P:P + 1], min_val=1, max_val=P // ET - 1)

            gathers, added = eng.alloc_register("gathers"), eng.alloc_register("added")
            eng.reg_mov(gathers, 1)
            eng.reg_mov(added, 16)

            def gather(s, t):
                eng.wait_ge(s_ix, gathers)
                eng.reg_add(gathers, gathers, 1)
                eng.wait_ge(s_meta, 1)
                eng.indirect_dma_start(out=xg[s][:], out_offset=None, in_=h2_d,
                                       in_offset=bass.IndirectOffsetOnAxis(ap=ix[s][:, 0:1], axis=0)
                                       ).then_inc(s_ga[s], 16)
            gather(0, 0)
            gather(1, 1)
            for i in range(2):
                eng.wait_ge(s_yw[i], 16 * (3 - i))
            with eng.Fori(0, groups) as i:
                for s in range(ET):
                    t = ET * i + s
                    eng.wait_ge(s_tp, 2 * t + 2)
                    eng.wait_ge(s_gc, t + 1)
                    gather(s, t + 2)
                    eng.wait_ge(s_ya, t + 2)
                    eng.wait_ge(s_yd, t + 2)
                    eng.wait_ge(s_ixs, t + 1)
                    eng.wait_ge(s_sca, added)
                    eng.reg_add(added, added, 16)
                    eng.wait_ge(s_meta, 1)
                    eng.indirect_dma_start(out=y_d, out_offset=bass.IndirectOffsetOnAxis(ap=ixs[s][:, 0:1], axis=0),
                                           in_=yo[s][:], in_offset=None, compute_op=ALU.add).then_inc(s_sca, 16)
            eng.wait_ge(s_sca, 16 * ET * groups + 16)
            for s in range(ET):
                eng.wait_ge(s_ga[s], 16 * (groups + 1))
            eng.nop().then_inc(s_all, 1)

        @block.scalar
        def _(eng):
            eng.wait_ge(s_in, 16 * 4)
            eng.activation(csig[:], crow[:], ACT.Sigmoid).then_inc(s_csig, 1)
            eng.wait_ge(s_cT, 2)
            eng.activation(cT[:], pb[6][:, 0:72], ACT.Copy).then_inc(s_smallT, 1)
            eng.activation(t19[:].rearrange("p a b -> p (a b)"), pb[6][:, 192:230], ACT.Copy).then_inc(s_smallT, 1)
            for i in range(ADA_1):
                half, c0 = 1 - ADA_W * i // D, ADA_W * i % D
                eng.wait_ge(s_each, i + 1)
                eng.activation(m1[0][half][:, c0:c0 + ADA_W], pb[6 + i % 2][:, 0:ADA_W], ACT.Copy)
                eng.activation(m1[1][half][0:NS, c0:c0 + ADA_W], pb[6 + i % 2][0:NS, ADA_W:2 * ADA_W],
                               ACT.Copy).then_inc(s_m1, 1)
                j = i - 2
                if 0 <= j < TILES:
                    if j:
                        eng.wait_ge(s_ss1, j)
                    else:
                        eng.wait_ge(s_x, 16 * TILES)
                        eng.wait_ge(s_var1, 1)
                    eng.activation(junk[0:nt(j), :], x_t[0:nt(j), j, :], ACT.Square,
                                   accum_out=ss1[0:nt(j), j:j + 1]).then_inc(s_ss1, 1)
            eng.wait_ge(s_var1, 2)
            eng.activation(rs1, ss1, ACT.Sqrt).then_inc(s_sd1, 1)
            for q in range(9):
                eng.wait_ge(s_bmm, q + 1)
                if q < 5:
                    w = 512 if q < 4 else 256
                    eng.activation(bv[:, 512 * q:512 * q + w], pb[q % 4][0:G * H, 0:w], ACT.Copy).then_inc(s_bev, 1)
                else:
                    eng.activation(bs[:, SW * (q - 5):SW * (q - 4)], pb[q % 4][0:G * H, 0:SW],
                                   ACT.Copy).then_inc(s_bev, 1)
            for j, tt in enumerate(ORDER):
                for half in range(2):
                    eng.wait_ge(s_hTp, 2 * j + half + 1)
                    n = nt(tt)
                    eng.activation(hT[:, 4 * half:4 * half + 4, tok(tt)],
                                   pb[2 + half][:, 0:4 * n].rearrange("p (k n) -> p k n", k=4),
                                   ACT.Copy).then_inc(s_hT, 1)

            def qk_out(z):
                c, tt = z // 5, ORDER[z % 5]
                n = nt(tt)
                eng.wait_ge(s_qkp, z + 1)
                dst = (qT, kT)[c // 2][:, 3 * (c % 2):3 * (c % 2) + 3, tok(tt)]
                eng.activation(dst, pb[2 + z % 2][:, 0:3 * n].rearrange("p (k n) -> p k n", k=3),
                               ACT.Copy).then_inc(s_qk, 1)
                if tt == SAMPLE:
                    eng.dma_start(new_d[c // 2, :, PJ_W * (c % 2):PJ_W * (c % 2 + 1)], kn[z % 3][0:NS, :]
                                  ).then_inc(s_qout if c < 2 else s_kout[z % 3], 16)
                elif c >= 2:
                    for g, lo, hi in KSEG[c % 2]:
                        skip = max(0, SEQ - WB[g]) // DIL
                        base = PJ_W * (c % 2) - GW * g
                        dst = k_prompt[g].rearrange("z y (l r) h d -> (z y r) l (h d)", r=DIL)[tt]
                        eng.dma_start(dst[:, base + lo:base + hi], kn[z % 3][skip:P, lo:hi]
                                      ).then_inc(s_kout[z % 3], 16)

            for c in range(8):
                for j, tt in enumerate(ORDER if c < 6 else range(3)):
                    n = nt(tt)
                    z = 5 * c + j if c < 6 else 30 + 3 * (c - 6) + j
                    if z < 20:
                        eng.wait_ge(s_pj, z + 1)
                        if z >= 2:
                            eng.wait_ge(s_var, z - 1)
                        eng.activation(sq[z % 2][0:n, :], pb[z % 2][0:n, 0:PJ_W], ACT.Square).then_inc(s_sq, 1)
                        eng.wait_ge(s_var, z + 1)
                        eng.activation(ssq[z % 2][0:n, :], ssq[z % 2][0:n, :], ACT.Sqrt).then_inc(s_sd, 1)
                    elif z < 30:
                        eng.wait_ge(s_pj, z + 1)
                        eng.activation(v_r[0:n, tt, PJ_W * (c - 4):PJ_W * (c - 3)], pb[z % 2][0:n, 0:PJ_W],
                                       ACT.Copy).then_inc(s_pjv, 1)
                    elif z < 34:
                        eng.wait_ge(s_pj, z + 1)
                        dst = (uT, gT)[(z - 30) // 2][:, z % 2, :]
                        eng.activation(dst[:, 0:SEQ], pb[z % 2][:, :], ACT.Copy)
                        eng.activation(dst[:, SEQ:NTOK], pb[2 + z % 2][:, 0:NS], ACT.Copy).then_inc(s_pjv, 1)
                    if 1 <= z <= 20:
                        if z == 1:
                            eng.wait_ge(s_bvw, 16)
                        qk_out(z - 1)
                    if 2 <= z < 2 + len(copies):
                        eng.dma_start(*copies[z - 2]).then_inc(s_caches, 16)
            eng.wait_ge(s_snew, 1)
            for o in range(2):
                eng.activation(stn[:].rearrange("p g (e o n) -> p o g e n", e=2, o=2)[:, o],
                               pb[6 + o][0:NS, 0:2 * NS * G].rearrange("p (g e n) -> p g e n", g=G, e=2),
                               ACT.Copy).then_inc(s_snT, 1)
            eng.wait_ge(s_csT, 1)
            eng.activation(cso[:], pb[5][0:18, 0:CC], ACT.Copy).then_inc(s_cso, 1)
            eng.wait_ge(s_cso, 1)
            eng.dma_start(conv_p.rearrange("z y j c -> (z y j) c"), cso[0:2, :]).then_inc(s_cout, 16)
            eng.dma_start(conv_s.rearrange("z b j c -> (z b j) c"), cso[2:18, :]).then_inc(s_cout, 16)
            eng.wait_ge(s_smx, 1)
            eng.activation(sp[:], sp[:], ACT.Exp, bias=snm, accum_out=szs).then_inc(s_sex, 1)
            for u in range(18):
                if u < 16:
                    eng.wait_ge(s_mx, u + 1)
                    i = u % 2
                    eng.activation(sc_t[i][:], sc_t[i][:], ACT.Exp, bias=nmx[:, i:i + 1],
                                   accum_out=zs[:, i:i + 1]).then_inc(s_ex, 1)
                if u >= 2:
                    h, r = (u - 2) // 4, (u - 2) % 4
                    hb = DH * (h % 2)
                    eng.wait_ge(s_O, u - 1)
                    eng.activation(catT[hb:hb + DH, 0:6, P * r:P * (r + 1)].rearrange("p (g e) n -> p e g n", e=2)[:, h // 2],
                                   pb[6][hb:hb + DH, 0:G * P].rearrange("p (g n) -> p g n", g=G),
                                   ACT.Copy).then_inc(s_Oe, 1)
                if u == 1:
                    eng.wait_ge(s_sPTp, 1)
                    eng.activation(spT[:, 0:2, :], pb[7][:, 0:256].rearrange("p (a b) -> p a b", a=2), ACT.Copy)
                    eng.activation(spT[0:64, 2, :], pb[7][0:64, 256:384], ACT.Copy).then_inc(s_sPT, 1)
                if u == 2:
                    eng.wait_ge(s_sPTp, 2)
                    eng.activation(spT[0:NS, 3:6, :], pb[7][0:NS, 0:384].rearrange("p (a b) -> p a b", a=3),
                                   ACT.Copy).then_inc(s_sPT, 1)
                if 1 <= u <= 16:
                    i = (u - 1) % 2
                    if u == 1:
                        eng.wait_ge(s_cout, 32)
                    eng.wait_ge(s_Tp, 2 * u - 1)
                    if u >= 3:
                        eng.wait_ge(s_O, u - 2)
                    eng.activation(pT_t[i][:, 0:512], pb[4][:, :], ACT.Copy).then_inc(s_T, 1)
                    eng.wait_ge(s_Tp, 2 * u)
                    eng.activation(pT_t[i][:, 512:768], pb[5][:, 0:256], ACT.Copy).then_inc(s_T, 1)
            eng.wait_ge(s_spv, G * B)
            for hh in range(2):
                o = pb[7][DH * hh:DH * (hh + 1), 0:384].rearrange("p (q s n) -> p s q n", q=6, s=2)[:, hh]
                eng.activation(catT[DH * hh:DH * (hh + 1), 0:6, SEQ:NTOK], o, ACT.Copy).then_inc(s_sO, 1)
            for j, tt in enumerate(ORDER):
                eng.wait_ge(s_x1, 10 + j + 1)
                if j:
                    eng.wait_ge(s_ss2, j)
                eng.activation(junk[0:nt(tt), :], x_t[0:nt(tt), tt, :], ACT.Square,
                               accum_out=ss2[0:nt(tt), tt:tt + 1]).then_inc(s_ss2, 1)
                eng.wait_ge(s_var2, j + 1)
                eng.activation(rs2[0:nt(tt), tt:tt + 1], ss2[0:nt(tt), tt:tt + 1], ACT.Sqrt).then_inc(s_sd2, 1)
            eng.wait_ge(s_rz, 1)

            def sigmoid(j):
                tt = ORDER[j]
                eng.wait_ge(s_lg, j + 1)
                eng.activation(r_sc[0:nt(tt), NE * tt:NE * (tt + 1)], pb[4 + j % 2][0:nt(tt), 0:NE], ACT.Sigmoid
                               ).then_inc(s_sc, 1)
            for j, tt in enumerate(ORDER):
                n = nt(tt)
                for half in range(2):
                    eng.wait_ge(s_h2p, 2 * j + half + 1)
                    eng.activation(h2T[:, 4 * half:4 * half + 4, tok(tt)],
                                   pb[2 + half][:, 0:4 * n].rearrange("p (k n) -> p k n", k=4),
                                   ACT.Copy).then_inc(s_h2T, 1)
                if j:
                    sigmoid(j - 1)
            sigmoid(TILES - 1)
            for f in range(2):
                eng.wait_ge(s_su, 2 * f + 1)
                eng.activation(sg[:, f, 0:SEQ], pb[4 * f][:, :], ACT.Silu)
                eng.activation(sg[:, f, SEQ:NTOK], pb[4 * f + 2][:, 0:NS], ACT.Silu).then_inc(s_sg, 1)
            for j, tt in enumerate(ORDER):
                if j >= 2:
                    eng.wait_ge(s_yw[j % 2], 16 * (j // 2))
                for half in range(2):
                    u = 2 * j + half
                    eng.wait_ge(s_sd_, u + 1)
                    eng.activation(y_row[j % 2][0:nt(tt), 512 * half:512 * half + 512], pb[YB[u % 4]][0:nt(tt), :],
                                   ACT.Copy).then_inc(s_ysh, 1)
                eng.wait_ge(s_ysh, 2 * j + 2)
                eng.dma_start(y_d[tok(tt), :], y_row[j % 2][0:nt(tt), :]).then_inc(s_yw[j % 2], 16)
            eng.wait_ge(s_meta, 1)
            groups = eng.value_load(meta[0:1, P:P + 1], min_val=1, max_val=P // ET - 1)

            def x_evac(s, t):
                eng.wait_ge(s_tp, 2 * t + 1)
                eng.activation(xT[s][:, 0:4, :], pb[4][:, :].rearrange("p (k n) -> p k n", k=4), ACT.Copy
                               ).then_inc(s_xa, 1)
            x_evac(0, 0)
            eng.nop().then_inc(s_ya, 1)
            for i in range(2):
                eng.wait_ge(s_yw[i], 16 * (3 - i))
            with eng.Fori(0, groups) as i:
                for s in range(ET):
                    t = ET * i + s
                    eng.wait_ge(s_upg, t + 1)
                    eng.wait_ge(s_he, t + 1)
                    eng.activation(sge[s], pb[0][:, 0:2 * P].rearrange("p (f n) -> p f n", f=2), ACT.Silu
                                   ).then_inc(s_si, 1)
                    x_evac(1 - s, t + 1)
                    eng.wait_ge(s_dn, 2 * ET + 2 * t + 1)
                    eng.wait_ge(s_gc, t + 1)
                    eng.wait_ge(s_ixs, t + 1)
                    eng.activation(yo[s][:, 0:512], pb[2][:, :], ACT.Copy, scale=gcol[s]).then_inc(s_ya, 1)

        @block.tensor
        def _(eng):
            ident, flip = const("ident"), const("flip")

            def turn(dst, src, parts):
                return eng.transpose(dst, src, ident[0:parts, 0:parts])

            def ring_in(n):
                eng.wait_ge(s_ring[n % RING], landed[n])

            eng.wait_ge(s_cst, 16)
            eng.wait_ge(s_cs, 1)
            for k in range(KD):
                last = turn(pb[6][:, 9 * k:9 * k + 9], csig[:, P * k:P * (k + 1)], 9)
            last.then_inc(s_cT, 1)
            turn(pb[6][:, 192:211], rows19[:, 0:P], 19)
            turn(pb[6][:, 211:230], rows19[:, P:CC], 19).then_inc(s_cT, 1)

            def ada(i):
                n = ring_uses("ada", i)
                ring_in(n)
                w = ring[n % RING][:, 0:KD * ADA_W].rearrange("p (k n) -> p k n", k=KD)
                if i >= 2:
                    eng.wait_ge(s_mrow, i - 1)
                for k in range(KD):
                    mm = eng.matmul(pb[4 + i % 2][0:1 + B, 0:ADA_W], lhsT=cT[:, 9 * k:9 * k + 9], rhs=w[:, k, :],
                                    start=(k == 0), stop=(k == KD - 1))
                mm.then_inc(s_ada, 1)

            def to_tokens(i):
                eng.wait_ge(s_mrow, i + 1)
                if i >= 2:
                    eng.wait_ge(s_m1, i - 1)
                each = const("each", parts=1 + B)
                eng.matmul(pb[6 + i % 2][:, 0:ADA_W], lhsT=each[:, 0:P], rhs=mrow[:, i % 4, :], start=True, stop=True)
                eng.matmul(pb[6 + i % 2][0:NS, ADA_W:2 * ADA_W], lhsT=each[:, P:P + NS], rhs=mrow[:, i % 4, :],
                           start=True, stop=True).then_inc(s_each, 1)

            eng.wait_ge(s_smallT, 2)
            for i in range(ADA_1):
                ada(i)
                if i:
                    to_tokens(i - 1)
            to_tokens(ADA_1 - 1)
            eng.wait_ge(s_oh, 64)
            for q in range(9):
                if q >= 4:
                    eng.wait_ge(s_bev, q - 3)
                if q < 5:
                    w = 512 if q < 4 else 256
                    mm = eng.matmul(pb[q % 4][0:G * H, 0:w], lhsT=relb[:], rhs=ohp[:, 512 * q:512 * q + w],
                                    start=True, stop=True)
                else:
                    mm = eng.matmul(pb[q % 4][0:G * H, 0:SW], lhsT=relb[0:32, :], rhs=ohs[:, SW * (q - 5):SW * (q - 4)],
                                    start=True, stop=True)
                mm.then_inc(s_bmm, 1)
            eng.wait_ge(s_bev, 9)
            eng.wait_ge(s_m1, ADA_1)
            for g in range(G):
                for t in range(T):
                    c0 = SW * t + SOFF[g]
                    mm = eng.matmul(pb[7][:, SOFF[g]:SOFF[g] + SEG[g]], lhsT=sel[:, g, t, :], rhs=bs[:, c0:c0 + SEG[g]],
                                    start=(t == 0), stop=(t == T - 1))
            mm.then_inc(s_tsmm, 1)
            for j, tt in enumerate(ORDER):
                n = nt(tt)
                eng.wait_ge(s_h, j + 1)
                for k in range(KD):
                    if k % 4 == 0 and j:
                        eng.wait_ge(s_hT, 2 * j - 1 + k // 4)
                    mm = turn(pb[2 + k // 4][:, n * (k % 4):n * (k % 4 + 1)], h_row[j % 2][0:n, P * k:P * (k + 1)], n)
                    if k % 4 == 3:
                        mm.then_inc(s_hTp, 1)

            def qk_turn(z):
                tt = ORDER[z % 5]
                n = nt(tt)
                eng.wait_ge(s_kn, z + 1)
                if z >= 2:
                    eng.wait_ge(s_qk, z - 1)
                for m in range(3):
                    to, rows = pb[2 + z % 2][:, n * m:n * (m + 1)], kn[z % 3][0:n, P * m:P * (m + 1)]
                    if z < 10 and tt != SAMPLE:
                        last = eng.matmul(to, lhsT=rows, rhs=flip, start=True, stop=True)
                    else:
                        last = turn(to, rows, n)
                last.then_inc(s_qkp, 1)

            eng.wait_ge(s_hT, 2 * TILES)
            for c in range(8):
                n = ring_uses("proj", c)
                ring_in(n)
                w = ring[n % RING].rearrange("p (k n) -> p k n", k=KD)
                for j, tt in enumerate(ORDER if c < 6 else range(3)):
                    z = 5 * c + j if c < 6 else 30 + 3 * (c - 6) + j
                    if z >= 2:
                        eng.wait_ge(*evac_count(z - 2))
                    if c < 6:
                        for k in range(KD):
                            mm = eng.matmul(pb[z % 2][0:nt(tt), 0:PJ_W], lhsT=hT[:, k, tok(tt)], rhs=w[:, k, :],
                                            start=(k == 0), stop=(k == KD - 1))
                    else:
                        for k in range(KD):
                            eng.matmul(pb[z % 2][:, :], lhsT=w[:, k, P * j:P * (j + 1)], rhs=hT[:, k, 0:SEQ],
                                       start=(k == 0), stop=(k == KD - 1))
                        for k in range(KD):
                            mm = eng.matmul(pb[2 + z % 2][:, 0:NS], lhsT=w[:, k, P * j:P * (j + 1)],
                                            rhs=hT[:, k, SEQ:NTOK], start=(k == 0), stop=(k == KD - 1))
                    mm.then_inc(s_pj, 1)
                    if 1 <= z <= 20:
                        qk_turn(z - 1)
                    if z == 29:
                        eng.wait_ge(s_qk, 20)
                ada(ADA_1 + 2 * c)
                ada(ADA_1 + 2 * c + 1)
            eng.wait_ge(s_mrow, ADA_N)
            for h in (0, 2, 1, 3):
                for g in range(G):
                    hb, q = DH * (h % 2), 2 * g + h // 2
                    c0 = 2 * NS * g + NS * (h // 2)
                    mm = eng.matmul(pb[6 + h % 2][0:NS, c0:c0 + NS], lhsT=kT[hb:hb + DH, q, SEQ:NTOK],
                                    rhs=qT[hb:hb + DH, q, SEQ:NTOK], start=True, stop=True)
            mm.then_inc(s_snew, 1)
            eng.wait_ge(s_csx, 2)
            eng.wait_ge(s_mrow, ADA_N)
            turn(pb[5][0:18, 0:P], csx[:, 0, :], P)
            turn(pb[5][0:18, P:CC], csx[:, 1, :], P).then_inc(s_csT, 1)
            eng.wait_ge(s_sco, G * B)
            eng.wait_ge(s_snT, 2)
            for g in range(G):
                turn(pb[7][:, SOFF[g]:SOFF[g] + KEYS[g]], st[0:KEYS[g], g, :], KEYS[g])
                last = turn(pb[7][:, SOFF[g] + KEYS[g]:SOFF[g] + SEG[g]], stn[:, g, :], NS)
            last.then_inc(s_sS, 1)
            eng.wait_ge(s_cmul, 2)
            eng.wait_ge(s_cso, 1)
            for u in range(18):
                if u < 16:
                    h, r = u // 4, u % 4
                    hb, q = DH * (h % 2), h // 2
                    lo, hi = pb[2 * (u % 2)], pb[2 * (u % 2) + 1]
                    if u >= 2:
                        eng.wait_ge(s_add, u - 1)
                    eng.matmul(lo[:, :], lhsT=qT[hb:hb + DH, q, tok(r)], rhs=kT[hb:hb + DH, q, 0:SEQ],
                               start=True, stop=True)
                    for g in (1, 2):
                        mm = eng.matmul(hi[:, P * (g - 1):P * g], lhsT=qT[hb:hb + DH, 2 * g + q, tok(r)],
                                        rhs=kT[hb:hb + DH, 2 * g + q, tok(r)], start=True, stop=True)
                    mm.then_inc(s_S, 1)
                if u >= 2:
                    h, r = (u - 2) // 4, (u - 2) % 4
                    hb, pt = DH * (h % 2), pT_t[u % 2]
                    eng.wait_ge(s_T, 2 * (u - 1))
                    if u >= 3:
                        eng.wait_ge(s_Oe, u - 2)
                    for rk in range(DIL):
                        eng.matmul(pb[6][hb:hb + DH, 0:P], lhsT=v_r[:, rk, DH * h:DH * (h + 1)],
                                   rhs=pt[:, P * rk:P * (rk + 1)], start=(rk == 0), stop=(rk == DIL - 1))
                    for g in (1, 2):
                        mm = eng.matmul(pb[6][hb:hb + DH, P * g:P * (g + 1)],
                                        lhsT=v_r[:, r, GW * g + DH * h:GW * g + DH * (h + 1)],
                                        rhs=pt[:, P * (3 + g):P * (4 + g)], start=True, stop=True)
                    mm.then_inc(s_O, 1)
                if u == 1:
                    eng.wait_ge(s_sP, 1)
                    for g in range(G):
                        last = turn(pb[7][0:KEYS[g], P * g:P * (g + 1)], sp[:, SOFF[g]:SOFF[g] + KEYS[g]], P)
                    last.then_inc(s_sPTp, 1)
                if u == 2:
                    eng.wait_ge(s_sPT, 1)
                    for g in range(G):
                        last = turn(pb[7][0:NS, P * g:P * (g + 1)], sp[:, SOFF[g] + KEYS[g]:SOFF[g] + SEG[g]], P)
                    last.then_inc(s_sPTp, 1)
                if u == 3:
                    eng.wait_ge(s_sPT, 2)
                    for g in range(G):
                        for hp in range(2):
                            q = 2 * g + hp
                            eng.matmul(pb[7][:, 64 * q:64 * (q + 1)], lhsT=v_r[0:NS, SAMPLE, P * q:P * (q + 1)],
                                       rhs=spT[0:NS, 3 + g, 64 * hp:64 * (hp + 1)], start=(q == 0), stop=False,
                                       skip_group_check=True)
                if 3 <= u < 15:
                    for n in range(2 * (u - 3), 2 * (u - 2)):
                        g, b = sc_row(n)
                        w = KEYS[g]
                        eng.wait_ge(s_vb[n % VB], 16 * (n // VB + 1))
                        for hp in range(2):
                            q = 2 * g + hp
                            o = pb[7][:, 64 * q:64 * (q + 1)].rearrange("p (s n) -> p s n", s=2)
                            pr = spT[0:w, g, 64 * hp:64 * (hp + 1)].rearrange("p (s n) -> p s n", s=2)
                            if g == 0:
                                mm = eng.matmul(o[:, :, T * b:T * (b + 1)], lhsT=v_buf[n % VB][0:w, P * hp:P * (hp + 1)],
                                                rhs=pr[:, :, T * b:T * (b + 1)], start=False, stop=(n == 23),
                                                skip_group_check=True)
                            else:
                                for t in range(T):
                                    mm = eng.matmul(o[:, :, T * b + t:T * b + t + 1],
                                                    lhsT=v_buf[n % VB][0:w, GW * t + P * hp:GW * t + P * (hp + 1)],
                                                    rhs=pr[:, :, T * b + t:T * b + t + 1], start=False, stop=(n == 23),
                                                    skip_group_check=True)
                        mm.then_inc(s_spv, 1)
                if 1 <= u <= 16:
                    eng.wait_ge(s_P, u)
                    if u >= 2:
                        eng.wait_ge(s_T, 2 * (u - 1))
                    for m in range(6):
                        mm = eng.matmul((pb[4][:, P * m:P * (m + 1)] if m < 4 else pb[5][:, P * (m - 4):P * (m - 3)]),
                                        lhsT=sc_t[(u - 1) % 2][:, P * m:P * (m + 1)], rhs=flip, start=True, stop=True)
                        if m in (3, 5):
                            mm.then_inc(s_Tp, 1)
            eng.wait_ge(s_Oe, 16)
            eng.wait_ge(s_sO, 2)
            eng.wait_ge(s_conv, 4)
            eng.wait_ge(s_add, 16)
            for o in range(3):
                n = ring_uses("wo", o)
                ring_in(n)
                w = ring[n % RING][:, 0:KD * WO_W[o]].rearrange("p (k n) -> p k n", k=KD)
                for j, tt in enumerate(ORDER):
                    u = 5 * o + j
                    if u >= 2:
                        eng.wait_ge(s_wg, u - 1)
                    for k in range(KD):
                        mm = eng.matmul(pb[u % 2][0:nt(tt), 0:WO_W[o]], lhsT=catT[:, k, tok(tt)], rhs=w[:, k, :],
                                        start=(k == 0), stop=(k == KD - 1))
                    mm.then_inc(s_wo, 1)
            eng.wait_ge(s_wr, 16)

            def router(j):
                tt = ORDER[j]
                eng.wait_ge(s_h2T, 2 * j + 2)
                if j >= 2:
                    eng.wait_ge(s_sc, j - 1)
                for k in range(KD):
                    mm = eng.matmul(pb[4 + j % 2][0:nt(tt), 0:NE], lhsT=h2T[:, k, tok(tt)], rhs=wr[:, k, :],
                                    start=(k == 0), stop=(k == KD - 1))
                mm.then_inc(s_lg, 1)
            for j, tt in enumerate(ORDER):
                n = nt(tt)
                eng.wait_ge(s_h2, j + 1)
                for k in range(KD):
                    if k % 4 == 0 and j:
                        eng.wait_ge(s_h2T, 2 * j - 1 + k // 4)
                    mm = turn(pb[2 + k // 4][:, n * (k % 4):n * (k % 4 + 1)], h2_row[j % 2][0:n, P * k:P * (k + 1)], n)
                    if k % 4 == 3:
                        mm.then_inc(s_h2p, 1)
                if j:
                    router(j - 1)
            router(TILES - 1)
            n_g, n_u, n_d = (ring_uses(k, 0) for k in ("sgate", "sup", "sdown"))
            eng.wait_ge(s_wg, 15)
            eng.wait_ge(s_h2T, 2 * TILES)
            ring_in(n_g)
            ring_in(n_u)
            upper, ones = const("upper"), const("ones")

            def ranks():
                eng.wait_ge(s_M, 1)
                eng.wait_ge(s_hs, 1)
                for k in range(TILES):
                    for j in range(k + 1):
                        eng.matmul(pb[3][:, NE * k:NE * (k + 1)], lhsT=upper if j == k else ones,
                                   rhs=r_m[:, NE * j:NE * (j + 1)], start=(j == 0), stop=(j == k))
                for j in range(TILES):
                    mm = eng.matmul(pb[3][:, RW:RW + NE], lhsT=ones, rhs=r_m[:, NE * j:NE * (j + 1)],
                                    start=(j == 0), stop=(j == TILES - 1))
                mm.then_inc(s_rank, 1)

            for f in range(2):
                if f:
                    ranks()
                    eng.wait_ge(s_sc, TILES)
                for q, n in ((0, n_g), (1, n_u)):
                    if f and q:
                        eng.wait_ge(s_ecol, 1)
                        turn(pb[3][0:1, RW:RW + P], ecol[:], P).then_inc(s_eT, 1)
                    w = ring[n % RING][:, 0:KD * FE].rearrange("p (k n) -> p k n", k=KD)
                    for k in range(KD):
                        eng.matmul(pb[4 * f + q][:, :], lhsT=w[:, k, P * f:P * (f + 1)], rhs=h2T[:, k, 0:SEQ],
                                   start=(k == 0), stop=(k == KD - 1))
                    for k in range(KD):
                        mm = eng.matmul(pb[4 * f + q + 2][:, 0:NS], lhsT=w[:, k, P * f:P * (f + 1)],
                                        rhs=h2T[:, k, SEQ:NTOK], start=(k == 0), stop=(k == KD - 1))
                    mm.then_inc(s_su, 1)
            for s in range(ET):
                eng.nop().then_inc(s_up, 1)
                eng.nop().then_inc(s_dn, 1)
                eng.nop().then_inc(s_dn, 1)
            ring_in(n_d)
            wd = ring[n_d % RING][:, 0:2 * D].rearrange("p (k n) -> p k n", k=2)
            eng.wait_ge(s_hs, 2)

            def shared_down(u):
                tt, half = ORDER[u // 2], u % 2
                if u >= 4:
                    eng.wait_ge(s_ysh, u - 3)
                for f in range(2):
                    mm = eng.matmul(pb[YB[u % 4]][0:nt(tt), :], lhsT=hs[:, f, tok(tt)], rhs=wd[:, f, 512 * half:512 * half + 512],
                                    start=(f == 0), stop=(f == 1))
                mm.then_inc(s_sd_, 1)
            eng.wait_ge(s_meta, 1)
            groups = eng.value_load(meta[0:1, P:P + 1], min_val=1, max_val=P // ET - 1)

            def slots(s, t):
                eng.wait_ge(s_oneh, t + 1)
                for k in range(TILES):
                    mm = eng.matmul(pb[6][:, 0:3], lhsT=oneh[s][:, k, :], rhs=slotb[:, 3 * k:3 * k + 3],
                                    start=(k == 0), stop=(k == TILES - 1))
                mm.then_inc(s_im, 1)

            for u in range(10):
                shared_down(u)
                if u == 0:
                    slots(0, 0)
                if u == 2:
                    eng.wait_ge(s_ix, 1)
                    slots(1, 1)
            eng.wait_ge(s_ysh, 10)

            def x_turn(s, t, uses):
                eng.wait_ge(s_ga[s], 16 * uses)
                for k in range(KD):
                    mm = turn(pb[4 + k // 4][:, P * (k % 4):P * (k % 4 + 1)], xg[s][:, P * k:P * (k + 1)], P)
                    if k % 4 == 3:
                        mm.then_inc(s_tp, 1)
            x_turn(0, 0, 1)
            with eng.Fori(0, groups) as i:
                for s in range(ET):
                    t = ET * i + s
                    eng.wait_ge(s_wgu[s], 32 * i + 32)
                    eng.wait_ge(s_xa, t + 1)
                    eng.wait_ge(s_xd, t + 1)
                    for q in range(2):
                        for f in range(2):
                            for k in range(KD):
                                mm = eng.matmul(pb[q][:, P * f:P * (f + 1)], lhsT=wgu[s][:, q, k, P * f:P * (f + 1)],
                                                rhs=xT[s][:, k, :], start=(k == 0), stop=(k == KD - 1))
                        mm.then_inc((s_upg, s_up)[q], 1)
                    eng.wait_ge(s_ix, t + 2)
                    slots(s, t + 2)
                    x_turn(1 - s, t + 1, i + 1 + s)
                    eng.wait_ge(s_he, t + 2)
                    eng.wait_ge(s_wdn[s], 16 * i + 16)
                    eng.wait_ge(s_ya, t + 1)
                    eng.wait_ge(s_yd, t + 1)
                    for half in range(2):
                        for f in range(2):
                            mm = eng.matmul(pb[2 + half][:, :], lhsT=he[s][:, f, :],
                                            rhs=wdn[s][:, f, 512 * half:512 * half + 512], start=(f == 0), stop=(f == 1))
                        mm.then_inc(s_dn, 1)

        @block.vector
        def _(eng):
            links = [0]

            def link(ins):
                links[0] += 1
                ins.then_inc(s_link, 1)
                eng.wait_ge(s_link, links[0])

            link(eng.memset(ss1, 1.0))
            link(eng.memset(ss2, 1.0))
            eng.wait_ge(s_csig, 1)
            eng.tensor_tensor(csig[:], csig[:], crow[:], ALU.mult).then_inc(s_cs, 1)
            eng.nop().then_inc(s_var1, 1)
            eng.wait_ge(s_smallT, 2)
            for m in range(2):
                link(eng.tensor_copy(upS[:, m, :, 0:2], t19[:, m, 0:16].rearrange("p (b j) -> p b j", j=2)))
            eng.wait_ge(s_small, 48)
            link(eng.tensor_scalar(gq[:], gq[:], DH ** -0.5, None, ALU.mult))
            def ada_evac(i):
                n = ring_uses("ada", i)
                eng.wait_ge(s_ada, i + 1)
                if 4 <= i < ADA_1 + 4:
                    eng.wait_ge(s_each, i - 3)
                elif i >= 4:
                    eng.wait_ge(s_modw[i % 4], 16 * ((i - ADA_1) // 4))
                dst = mrow[:, i % 4, :]
                add = eng.tensor_tensor(dst, pb[4 + i % 2][0:1 + B, 0:ADA_W], ada_row(n, 0), ALU.add)
                if scale_of(i):
                    link(add)
                    add = eng.scalar_tensor_tensor(out=dst, in0=dst, scalar=1.0, in1=ada_row(n, 1), op0=ALU.add,
                                                   op1=ALU.mult)
                add.then_inc(s_mrow, 1)

            for i in range(ADA_1):
                ada_evac(i)
            eng.wait_ge(s_ss1, TILES)
            eng.tensor_scalar(ss1, ss1, 1.0 / D, EPS, ALU.mult, ALU.add).then_inc(s_var1, 1)
            eng.wait_ge(s_sd1, 1)
            link(eng.reciprocal(rs1, rs1))
            eng.wait_ge(s_m1, ADA_1)
            for j, tt in enumerate(ORDER):
                n, s = nt(tt), int(tt == SAMPLE)
                if j == 2:
                    eng.wait_ge(s_tsmm, 1)
                    eng.tensor_tensor(ts[:], pb[7][:, 0:SW], const("smask"), ALU.add).then_inc(s_ts, 1)
                if j >= 2:
                    eng.wait_ge(s_hTp, 2 * j - 2)
                link(eng.scalar_tensor_tensor(out=h_row[j % 2][0:n, :], in0=x_t[0:n, tt, :], scalar=rs1[0:n, tt:tt + 1],
                                              in1=m1[s][0][0:n, :], op0=ALU.mult, op1=ALU.mult))
                eng.tensor_tensor(h_row[j % 2][0:n, :], h_row[j % 2][0:n, :], m1[s][1][0:n, :], ALU.add
                                  ).then_inc(s_h, 1)

            def score(n):
                g, b = sc_row(n)
                w = KEYS[g]
                eng.wait_ge(s_kq[n % KB], 32 * (n // KB + 1))
                if n:
                    eng.wait_ge(s_sco, n)
                kk = k_buf[n % KB][0:w, 0:GW].unsqueeze(1).to_broadcast([w, T, GW]) if g == 0 else \
                    k_buf[n % KB][0:w, :].rearrange("p (t n) -> p t n", t=T)
                link(eng.tensor_tensor(prod[0:w, :].rearrange("p (t n) -> p t n", t=T), kk,
                                       q_buf[n % KB][0:w, :].rearrange("p (t n) -> p t n", t=T), ALU.mult))
                eng.tensor_reduce(st[0:w, g, :].rearrange("p (h b t) -> p b t h", h=H, b=B)[:, b],
                                  prod[0:w, :].rearrange("p (t h d) -> p t h d", t=T, h=H), AX, ALU.add
                                  ).then_inc(s_sco, 1)

            scored = 0
            for c in range(8):
                for j, tt in enumerate(ORDER if c < 6 else range(3)):
                    n = nt(tt)
                    z = 5 * c + j if c < 6 else 30 + 3 * (c - 6) + j
                    if z < 20:
                        i = z % 2
                        eng.wait_ge(s_sq, z + 1)
                        link(eng.tensor_reduce(ssq[i][0:n, :], sq[i][0:n, :].rearrange("p (h d) -> p h d", d=DH), AX,
                                               ALU.add))
                        eng.tensor_scalar(ssq[i][0:n, :], ssq[i][0:n, :], 1.0 / DH, EPS, ALU.mult, ALU.add
                                          ).then_inc(s_var, 1)
                        eng.wait_ge(s_sd, z + 1)
                        link(eng.reciprocal(ssq[i][0:n, :], ssq[i][0:n, :]))
                        if z >= 3:
                            eng.wait_ge(s_qkp, z - 2)
                            sem_out, val = KN_OUT[z - 3]
                            if sem_out is not None:
                                eng.wait_ge(s_qout if sem_out == "q" else s_kout[sem_out], val)
                        rows = kn[z % 3][0:n, :].rearrange("p (h d) -> p h d", d=DH)
                        eng.tensor_tensor(rows, pb[i][0:n, 0:PJ_W].rearrange("p (h d) -> p h d", d=DH),
                                          ssq[i][0:n, :].unsqueeze(2).to_broadcast([n, 6, DH]), ALU.mult
                                          ).then_inc(s_pjq, 1)
                        eng.wait_ge(s_pjq, z + 1)
                        gain = (gq if c < 2 else gk)[0:n, :].unsqueeze(1).to_broadcast([n, 6, DH])
                        eng.tensor_tensor(rows, rows, gain, ALU.mult).then_inc(s_kn, 1)
                    elif z == 30:
                        link(eng.memset(upP[:, :, 0:2], 0.0))
                    elif z >= 34:
                        m = z - 34
                        eng.wait_ge(s_pj, z + 1)
                        eng.wait_ge(s_pjv, 14)
                        nat = upP[:, m, 2:2 + SEQ].rearrange("p (l r) -> p r l", r=DIL)
                        eng.tensor_tensor(nat, pb[z % 2][:, :].rearrange("p (r l) -> p r l", r=DIL),
                                          uT[:, m, 0:SEQ].rearrange("p (r l) -> p r l", r=DIL), ALU.mult)
                        eng.tensor_tensor(upS[:, m, :, 2:2 + T], pb[2 + z % 2][:, 0:NS].rearrange("p (b t) -> p b t", t=T),
                                          uT[:, m, SEQ:NTOK].rearrange("p (b t) -> p b t", t=T), ALU.mult
                                          ).then_inc(s_cmul, 1)
                    if 10 <= z < 34:
                        score(scored)
                        scored += 1
                ada_evac(ADA_1 + 2 * c)
                ada_evac(ADA_1 + 2 * c + 1)
            assert scored == G * B
            eng.wait_ge(s_cmul, 2)
            for m in range(2):
                link(eng.tensor_copy(csx[:, m, 0:2], upP[:, m, SEQ:SEQ + 2]))
                eng.tensor_copy(csx[:, m, 2:18].rearrange("p (b j) -> p b j", j=2), upS[:, m, :, T:T + 2]
                                ).then_inc(s_csx, 1)
            eng.wait_ge(s_csx, 2)
            cp = [at(m_kn, SEQ), at(m_kn + SEQ, SEQ)]
            cs_ = at(m_kn + 2 * SEQ, B, T)
            eng.wait_ge(s_qkp, 20)
            for i in range(3):
                eng.wait_ge(s_kout[i], KOUT[i])
            for m in range(2):
                w3 = t19[:, m, 16:19]
                link(eng.tensor_scalar(cp[0], upP[:, m, 0:SEQ], w3[:, 0:1], None, ALU.mult))
                link(eng.tensor_scalar(cs_, upS[:, m, :, 0:T], w3[:, 0:1], None, ALU.mult))
                for jj in (1, 2):
                    link(eng.scalar_tensor_tensor(out=cp[0], in0=upP[:, m, jj:jj + SEQ], scalar=w3[:, jj:jj + 1],
                                                  in1=cp[0], op0=ALU.mult, op1=ALU.add))
                    link(eng.scalar_tensor_tensor(out=cs_, in0=upS[:, m, :, jj:jj + T], scalar=w3[:, jj:jj + 1],
                                                  in1=cs_, op0=ALU.mult, op1=ALU.add))
                eng.tensor_tensor(catT[:, 6 + m, 0:SEQ].rearrange("p (r l) -> p r l", r=DIL),
                                  cp[0].rearrange("p (l r) -> p r l", r=DIL),
                                  gT[:, m, 0:SEQ].rearrange("p (r l) -> p r l", r=DIL), ALU.mult).then_inc(s_conv, 1)
                eng.tensor_tensor(catT[:, 6 + m, SEQ:NTOK], cs_.rearrange("p b t -> p (b t)"), gT[:, m, SEQ:NTOK],
                                  ALU.mult).then_inc(s_conv, 1)
                eng.wait_ge(s_conv, 2 * m + 2)
            eng.wait_ge(s_sS, 1)
            link(eng.tensor_tensor(sp[:], pb[7][:, 0:SW], ts[:], ALU.add))
            eng.tensor_reduce(snm, sp[:], AX, ALU.max, negate=True).then_inc(s_smx, 1)
            eng.wait_ge(s_sex, 1)
            link(eng.reciprocal(srz, szs))
            eng.tensor_scalar(sp[:], sp[:], srz, None, ALU.mult).then_inc(s_sP, 1)

            def norm(u):
                i = u % 2
                eng.wait_ge(s_ex, u + 1)
                link(eng.reciprocal(rz[:, i:i + 1], zs[:, i:i + 1]))
                eng.tensor_scalar(sc_t[i][:], sc_t[i][:], rz[:, i:i + 1], None, ALU.mult).then_inc(s_P, 1)

            for u in range(16):
                h, r, i = u // 4, u % 4, u % 2
                lo, hi = pb[2 * i], pb[2 * i + 1]
                eng.wait_ge(s_S, u + 1)
                if u >= 2:
                    eng.wait_ge(s_Tp, 2 * u - 2)
                if r == 0:
                    eng.wait_ge(s_tb[h % 2], 48 * (h // 2 + 1))
                tab = tb[h % 2]
                eng.tensor_tensor(sc_t[i][:, 0:512].rearrange("p (a b) -> p a b", a=4),
                                  lo[:, :].rearrange("p (a b) -> p a b", a=4), tab[:, 3 - r:7 - r, :], ALU.add)
                eng.tensor_tensor(sc_t[i][:, 512:768].rearrange("p (a b) -> p a b", a=2),
                                  hi[:, 0:256].rearrange("p (a b) -> p a b", a=2), tab[:, 7:9, :], ALU.add
                                  ).then_inc(s_add, 1)
                if u:
                    norm(u - 1)
                eng.wait_ge(s_add, u + 1)
                eng.tensor_reduce(nmx[:, i:i + 1], sc_t[i][:], AX, ALU.max, negate=True).then_inc(s_mx, 1)
            norm(15)
            def inverse_rms(j):
                tt = ORDER[j]
                n = nt(tt)
                eng.wait_ge(s_ss2, j + 1)
                eng.tensor_scalar(ss2[0:n, tt:tt + 1], ss2[0:n, tt:tt + 1], 1.0 / D, EPS, ALU.mult, ALU.add
                                  ).then_inc(s_var2, 1)
                eng.wait_ge(s_sd2, j + 1)
                link(eng.reciprocal(rs2[0:n, tt:tt + 1], rs2[0:n, tt:tt + 1]))

            def second_norm(j):
                tt = ORDER[j]
                n, s = nt(tt), int(tt == SAMPLE)
                if j >= 2:
                    eng.wait_ge(s_h2p, 2 * j - 2)
                    eng.wait_ge(s_h2w[j % 2], 16 * (j // 2))
                link(eng.scalar_tensor_tensor(out=h2_row[j % 2][0:n, :], in0=x_t[0:n, tt, :], scalar=rs2[0:n, tt:tt + 1],
                                              in1=m2[s][1][0:n, :], op0=ALU.mult, op1=ALU.mult))
                eng.tensor_tensor(h2_row[j % 2][0:n, :], h2_row[j % 2][0:n, :], m2[s][2][0:n, :], ALU.add
                                  ).then_inc(s_h2, 1)

            eng.wait_ge(s_m2, 16 * 3 * (T + 1))
            for o in range(3):
                c0, w = sum(WO_W[:o]), WO_W[o]
                for j, tt in enumerate(ORDER):
                    u, n, s = 5 * o + j, nt(tt), int(tt == SAMPLE)
                    eng.wait_ge(s_wo, u + 1)
                    eng.tensor_tensor(wt[u % 2][0:n, 0:w], pb[u % 2][0:n, 0:w], m2[s][0][0:n, c0:c0 + w], ALU.mult
                                      ).then_inc(s_wg, 1)
                    eng.wait_ge(s_wg, u + 1)
                    eng.tensor_tensor(x_t[0:n, tt, c0:c0 + w], x_t[0:n, tt, c0:c0 + w], wt[u % 2][0:n, 0:w], ALU.add
                                      ).then_inc(s_x1, 1)
                    if u in (12, 13):
                        inverse_rms(u - 12)
                        second_norm(u - 12)
            eng.wait_ge(s_vout, 16 * (DIL * G + 1))
            link(eng.memset(r_m, 0.0))
            eng.memset(r_sc, 0.0).then_inc(s_rz, 1)
            for j in range(2, TILES):
                inverse_rms(j)
            for j in range(2, TILES):
                second_norm(j)
            link(eng.tensor_copy(slotb[:, 0:15], const("slot")[:, 0:15]))
            eng.wait_ge(s_sc, TILES)

            def r3(v):
                return v.rearrange("p (k n) -> p k n", k=TILES)
            link(eng.tensor_tensor(r3(r_sel), r3(r_sc), br[:].unsqueeze(1).to_broadcast([P, TILES, NE]), ALU.add))
            for q in range(TILES * 8):
                last = eng.max(r_t8[:, 8 * q:8 * q + 8], r_sel[:, 8 * q:8 * q + 8])
            link(last)
            t8 = r_t8.rearrange("p (q n) -> p q n", n=8)
            link(eng.tensor_tensor(r_gs, t8[:, :, 0], t8[:, :, 1], ALU.add))
            gs = r_gs.rearrange("p (k g) -> p k g", k=TILES)
            other = gs.unsqueeze(2).to_broadcast([P, TILES, 8, 8])
            own = gs.unsqueeze(3).to_broadcast([P, TILES, 8, 8])

            def r4(v):
                return v.rearrange("p (k g h) -> p k g h", k=TILES, g=8)
            link(eng.tensor_tensor(r4(r_gt), other, own, ALU.is_gt))
            link(eng.tensor_tensor(r4(r_eq), other, own, ALU.is_equal))
            link(eng.tensor_tensor(r3(r_eq), r3(r_eq), const("tri8").unsqueeze(1).to_broadcast([P, TILES, 64]), ALU.mult))
            link(eng.tensor_tensor(r_gt, r_gt, r_eq, ALU.add))
            link(eng.tensor_reduce(r_rank, r_gt.rearrange("p (q n) -> p q n", n=8), AX, ALU.add))
            link(eng.tensor_scalar(r_gmb, r_rank, 3.5, NEG, ALU.is_ge, ALU.mult))
            link(eng.tensor_tensor(r_ma.rearrange("p (q n) -> p q n", n=8), r_sel.rearrange("p (q n) -> p q n", n=8),
                                   r_gmb.unsqueeze(2).to_broadcast([P, TILES * 8, 8]), ALU.add))
            for k in range(TILES):
                last = eng.max(r_top[:, k, :], r_ma[:, NE * k:NE * (k + 1)])
            link(last)
            for k in range(TILES):
                last = eng.match_replace(r_mr[:, NE * k:NE * (k + 1)], r_top[:, k, :], r_ma[:, NE * k:NE * (k + 1)], 2 * NEG)
            link(last)
            eng.tensor_tensor(r_m[:, 0:SAMPLE * NE], r_ma[:, 0:SAMPLE * NE], r_mr[:, 0:SAMPLE * NE], ALU.not_equal)
            eng.tensor_tensor(r_m[0:NS, SAMPLE * NE:RW], r_ma[0:NS, SAMPLE * NE:RW], r_mr[0:NS, SAMPLE * NE:RW],
                              ALU.not_equal).then_inc(s_M, 1)
            eng.wait_ge(s_M, 1)

            def shared_mul(f):
                eng.wait_ge(s_su, 2 * f + 2)
                eng.wait_ge(s_sg, f + 1)
                eng.tensor_tensor(hs[:, f, 0:SEQ], pb[4 * f + 1][:, :], sg[:, f, 0:SEQ], ALU.mult)
                eng.tensor_tensor(hs[:, f, SEQ:NTOK], pb[4 * f + 3][:, 0:NS], sg[:, f, SEQ:NTOK], ALU.mult
                                  ).then_inc(s_hs, 1)
            shared_mul(0)
            link(eng.tensor_tensor(r_g, r_sc, r_m, ALU.mult))
            link(eng.tensor_reduce(r_den, r3(r_g), AX, ALU.add))
            link(eng.tensor_scalar(r_den, r_den, 1e-30, None, ALU.max))
            link(eng.reciprocal(r_den, r_den))
            link(eng.tensor_scalar(r_den, r_den, 2.5, None, ALU.mult))
            eng.tensor_tensor(r3(r_g), r3(r_g), r_den.unsqueeze(2).to_broadcast([P, TILES, NE]), ALU.mult
                              ).then_inc(s_G, 1)
            eng.wait_ge(s_rank, 1)
            link(eng.tensor_copy(r_cnt, pb[3][:, RW:RW + NE]))
            link(eng.tensor_scalar(r_nt, r_cnt, 0.0, None, ALU.is_gt))
            for k in range(1, TILES):
                link(eng.scalar_tensor_tensor(out=r_nt, in0=r_cnt, scalar=float(P * k), in1=r_nt, op0=ALU.is_gt,
                                              op1=ALU.add))
            link(eng.tensor_tensor_scan(r_incl, const("ones")[:, 0:NE], r_nt, 0.0, ALU.mult, ALU.add))
            link(eng.tensor_scalar(r_cmp, r_incl, const("iotacol"), None, ALU.is_le))
            link(eng.tensor_reduce(ecol[:], r_cmp, AX, ALU.add))
            link(eng.tensor_scalar(ecol[:], ecol[:], float(NE - 1), None, ALU.min))
            link(eng.tensor_scalar(fpair, const("iota", parts=1), float(ET), r_incl[0:1, NE - 1:NE], ALU.mult, ALU.is_lt))
            link(eng.tensor_reduce(fcnt[:], fpair, AX, ALU.add))
            link(eng.tensor_copy(meta[0:1, P:P + 1], fcnt[:]))
            link(eng.tensor_tensor(r_base, r_incl, r_nt, ALU.subtract))
            link(eng.tensor_scalar(r_base, r_base, float(P), 1.0, ALU.mult, ALU.add))
            link(eng.tensor_tensor(r3(r_pos), pb[3][:, 0:RW].rearrange("p (k n) -> p k n", k=TILES),
                                   r_base.unsqueeze(1).to_broadcast([P, TILES, NE]), ALU.add))
            eng.nop().then_inc(s_ecol, 1)
            link(eng.tensor_tensor(r_pos, r_pos, r_m, ALU.mult))
            link(eng.tensor_scalar(r_pos, r_pos, -1.0, None, ALU.add))
            eng.wait_ge(s_eT, 1)
            eng.tensor_copy(meta[0:1, 0:P], pb[3][0:1, RW:RW + P]).then_inc(s_meta, 1)
            eng.wait_ge(s_meta, 1)
            groups = eng.value_load(meta[0:1, P:P + 1], min_val=1, max_val=P // ET - 1)

            def one_hot(s, t):
                e = eng.value_load(meta[0:1, bass.ds(t, 1)], min_val=0, max_val=NE - 1)
                for k in range(TILES):
                    last = eng.tensor_scalar(oneh[s][:, k, :], const("iota"), r_pos[:, bass.ds(e + NE * k, 1)],
                                             const("negt")[:, bass.ds(t, 1)], ALU.subtract, ALU.is_equal)
                last.then_inc(s_oneh, 1)

            def rows(s, t):
                eng.wait_ge(s_im, t + 1)
                link_rows(eng.tensor_scalar(imt[:, 0:1], pb[6][:, 2:3], const("negdummy"), const("dummy"), ALU.mult,
                                            ALU.add), 2 * t + 1)
                link_rows(eng.tensor_tensor(imt[:, 1:2], imt[:, 0:1], pb[6][:, 0:1], ALU.add), 2 * t + 2)
                eng.tensor_tensor(ix[s], imt[:, 1:2], pb[6][:, 1:2], ALU.add).then_inc(s_ix, 1)

            def link_rows(ins, count):
                ins.then_inc(s_lrow, 1)
                eng.wait_ge(s_lrow, count)

            def x_evac(s, t, uses):
                eng.wait_ge(s_tp, 2 * t + 2)
                eng.tensor_copy(xT[s][:, 4:8, :], pb[5][:, :].rearrange("p (k n) -> p k n", k=4)).then_inc(s_xd, 1)
                e = eng.value_load(meta[0:1, bass.ds(t, 1)], min_val=0, max_val=NE - 1)
                eng.wait_ge(s_ga[s], 16 * uses)
                if not isinstance(t, int):
                    eng.wait_ge(s_ya, t)
                eng.tensor_copy(gcol[s], xg[s][:, bass.ds(e + D, 1)]).then_inc(s_gc, 1)

            one_hot(0, 0)
            one_hot(1, 1)
            shared_mul(1)
            rows(0, 0)
            rows(1, 1)
            x_evac(0, 0, 1)
            eng.nop().then_inc(s_he, 1)
            eng.nop().then_inc(s_yd, 1)
            eng.tensor_copy(ixs[0], ix[0]).then_inc(s_ixs, 1)
            for i in range(2):
                eng.wait_ge(s_yw[i], 16 * (3 - i))
            with eng.Fori(0, groups) as i:
                for s in range(ET):
                    t = ET * i + s
                    one_hot(s, t + 2)
                    eng.wait_ge(s_up, ET + t + 1)
                    eng.wait_ge(s_si, t + 1)
                    eng.wait_ge(s_dn, 2 * ET + 2 * t - 2)
                    eng.tensor_tensor(he[s], pb[1][:, 0:2 * P].rearrange("p (f n) -> p f n", f=2), sge[s], ALU.mult
                                      ).then_inc(s_he, 1)
                    rows(s, t + 2)
                    x_evac(1 - s, t + 1, i + 1 + s)
                    eng.wait_ge(s_dn, 2 * ET + 2 * t + 2)
                    eng.tensor_scalar(yo[s][:, 512:D], pb[3][:, :], gcol[s], None, ALU.mult).then_inc(s_yd, 1)
                    eng.wait_ge(s_sca, 16 * t + 16)
                    eng.tensor_copy(ixs[1 - s], ix[1 - s]).then_inc(s_ixs, 1)
            eng.wait_ge(s_g2, 16 * (T + 1))
            for j, tt in enumerate(ORDER):
                n, s = nt(tt), int(tt == SAMPLE)
                eng.wait_ge(s_yf[tt], 16)
                link(eng.tensor_tensor(yf[tt][0:n, :], yf[tt][0:n, :], g2[s][0:n, :], ALU.mult))
                eng.tensor_tensor(yf[tt][0:n, :], yf[tt][0:n, :], x_t[0:n, tt, :], ALU.add).then_inc(s_fin, 1)


_OUTS = ([(1, SEQ, D), (B, T, D)] + [(1, 1, min(w, SEQ), H, DH) for w in (128, 128, 512, 512, 2048, 2048)]
         + [(1, 1, 2, CC)] + [(1, B, min(w, 1024), H, DH) for w in (128, 128, 512, 512, 2048, 2048)]
         + [(1, B, 2, CC)])


def kernel(**inputs):
    import concourse.bacc as bacc
    from concourse.bass_utils import run_bass_kernel_spmd

    nc = bacc.Bacc("TRN2", target_bir_lowering=False, num_devices=1)
    arrays = {n: np.ascontiguousarray(x) for n, x in inputs.items()}
    arrays.update(constants())
    aps = {}
    feeds = {}
    for n, x in arrays.items():
        feeds[f"in_{n}"] = x
        aps[n] = nc.dram_tensor(f"in_{n}", x.shape, mybir.dt.from_np(x.dtype), kind="ExternalInput").ap()
    outs = [nc.dram_tensor(f"out_{i}", s, F32, kind="ExternalOutput").ap() for i, s in enumerate(_OUTS)]
    build(nc, aps, outs)
    r = run_bass_kernel_spmd(nc, [feeds], core_ids=[0])
    return tuple(r.results[0][f"out_{i}"] for i in range(len(_OUTS)))
```

```python
from contextlib import ExitStack

import numpy as np
import concourse.bass as bass
from concourse import mybir

F32 = mybir.dt.float32
BF16 = mybir.dt.bfloat16
I32 = mybir.dt.int32
ALU = mybir.AluOpType
ACT = mybir.ActivationFunctionType
AX = mybir.AxisListType.X

P = 128
D = 1024
KD = D // P
SEQ = 512
DIL = 4
PT_ = SEQ // DIL
B = 8
T = 4
NS = B * T
NTOK = SEQ + NS
TILES = 5
SAMPLE = 4
ORDER = [4, 0, 1, 2, 3]
G = 3
H = 4
DH = 64
GW = H * DH
AW = G * GW
CC = 256
NE = 64
FE = 256
NPROJ = 3 * AW + 3 * CC
WB = (128, 512, 1024)
DILS = (1, 4, 16)
STEPS = 128
NEG = -1.0e30
EPS = 1e-6
SEC = 6 * D
ADA_W = 256
ADA_N = SEC // ADA_W
ADA_1 = 2 * D // ADA_W
PJ_W = 384
WO_W = (384, 384, 256)
RING = 3
KB = 3
VB = 7
SLOT = KD * PJ_W
NVEC = 9
VL = 2 * P
KEYS = (128, 128, 64)
SEG = tuple(k + NS for k in KEYS)
SOFF = (0, SEG[0], SEG[0] + SEG[1])
SW = sum(SEG)
HROW = D + NE
TR = NTOK + P
ET = 2
MAXT = NE + NTOK * 8 // P + ET


def bucket(dist):
    if dist < 16:
        return dist
    large = 16 + int(np.float32(np.log(np.float32(dist) / np.float32(16))) / np.float32(np.log(2048 / 16))
                     * np.float32(16))
    return min(large, 31)


CST = {}
_off = 0
for _name, _w in (("ident", P), ("flip", P), ("iota", P), ("upper", P), ("ones", P), ("smask", SW), ("negt", P), ("slot", 16),
                  ("tri8", 64), ("dummy", 1), ("negdummy", 1), ("iotacol", 1), ("each", P + NS)):
    CST[_name] = (_off, _w)
    _off += _w
CSTW = _off


def constants():
    c = np.zeros((P, CSTW), np.float32)

    def put(name, a):
        o, w = CST[name]
        c[:, o:o + w] = a
    i = np.arange(P)
    put("ident", np.eye(P))
    put("flip", np.eye(P)[::-1])
    put("iota", np.broadcast_to(i, (P, P)))
    put("upper", i[:, None] < i[None, :])
    put("ones", 1.0)
    m = np.full((P, SW), NEG, np.float32)
    for p in range(P):
        b, t = (p % NS) // T, p % T
        for g in range(G):
            for l in range(KEYS[g]):
                if g > 0 or l >= t:
                    m[p, SOFF[g] + l] = 0.0
            for n in range(T):
                if (n <= t) if g == 0 else (n == t):
                    m[p, SOFF[g] + KEYS[g] + b * T + n] = 0.0
    put("smask", m)
    put("negt", np.broadcast_to(-P * i, (P, P)))
    s = np.zeros((P, 16), np.float32)
    for k in range(TILES):
        s[:, 3 * k] = P * k
        s[:, 3 * k + 1] = i
        s[:, 3 * k + 2] = 1.0
    put("slot", s)
    put("tri8", np.broadcast_to((np.arange(8)[None, :] < np.arange(8)[:, None]).reshape(-1), (P, 64)))
    put("dummy", (NTOK + i)[:, None])
    put("negdummy", -(NTOK + i)[:, None])
    put("iotacol", i[:, None])
    e = np.zeros((P, P + NS), np.float32)
    e[0, 0:P] = 1.0
    for b in range(B):
        e[1 + b, P + T * b:P + T * (b + 1)] = 1.0
    put("each", e)
    ohp = np.zeros((33, NVEC, VL), np.float32)
    for v in range(NVEC):
        for y in range(VL):
            x = 127 - y
            if v < 7:
                d = 4 * x + 3 - v
                step, dist = d, d
                ok = 0 <= d <= STEPS
            elif v == 7:
                dist, ok = 4 * x, x >= 0
            else:
                dist, ok = 4 * x, x >= 0 and x % 4 == 0
            if ok:
                ohp[bucket(dist), v, y] = 1.0
            else:
                ohp[32, v, y] = NEG
    ohs = np.zeros((32, T, SW), np.float32)
    for t in range(T):
        for g in range(G):
            for l in range(KEYS[g]):
                j = (STEPS + t - l) if g == 0 else (KEYS[g] - l)
                if 0 <= j <= STEPS:
                    ohs[bucket(j * DILS[g]), t, SOFF[g] + l] = 1.0
            for n in range(NS):
                j = (t - n % T) if g == 0 else 0
                if j >= 0:
                    ohs[bucket(j), t, SOFF[g] + KEYS[g] + n] = 1.0
    sel = np.zeros((G * H, G, T, P), np.float32)
    for g in range(G):
        for h in range(H):
            for p in range(P):
                if p // NS == h:
                    sel[g * H + h, g, p % T, p] = 1.0
    vm = np.zeros((P, GW + B * 2 * T), np.float32)
    for p in range(P):
        t, h, b = p // NS, p % NS // B, p % B
        vm[p, DH * h:DH * (h + 1)] = 1.0
        for s_ in range(2):
            vm[p, GW + b * 2 * T + s_ * T + t] = 1.0
    return {"k_vm": vm, "k_cst": c, "k_ohp": ohp.reshape(33, -1), "k_ohs": ohs.reshape(32, -1), "k_sel": sel.reshape(G * H, -1)}


KSEG = (((0, 0, 256), (1, 256, 384)), ((1, 0, 128), (2, 128, 384)))


def row_writes():
    out, total, sample_q = [], [0, 0, 0], 0
    for z in range(20):
        sample = ORDER[z % 5] == SAMPLE
        if z < 10:
            sample_q += 16 * sample
            out.append(("q", sample_q) if sample else (None, 0))
        else:
            total[z % 3] += 16 if sample else 32
            out.append((z % 3, total[z % 3]))
    return out, total


KN_OUT, KOUT = row_writes()
WIDE = [(g, b) for g in (1, 2) for b in range(B)]
VUNITS = [WIDE[0]]
for _k in range(B):
    VUNITS += [WIDE[_k + 1], (0, _k)]
VUNITS += WIDE[B + 1:]
SPV = []
for _g, _b in VUNITS:
    SPV.append((SPV[-1] if SPV else 0) + (T if _g else 1))
FIRST_COPIES = 8
COPY_UNITS = (2, 5)
COPY_STEPS = range(4, 18, 2)
CONV = (14, 16)


def pj_done(z):
    return z + 1 + 3 * min(z // 5 + 1, 6)


def wo_done(u):
    return u + 1 + 3 * (u // 5 + 1)


YB = (0, 1, 4, 5)


def ring_items():
    items = [("ada", i) for i in range(ADA_1)]
    slots = [0, 1, 3, 4, 5, 2, 3, 4]
    assert len(slots) == ADA_1
    chunks = NPROJ // PJ_W
    items += [("proj", 0)]
    slots += [0]
    for c in range(chunks):
        if c + 1 < chunks:
            items += [("proj", c + 1)]
            slots += [(c + 1) % 2]
        items += [("ada", ADA_1 + 2 * c), ("ada", ADA_1 + 2 * c + 1)]
        slots += [2, 2]
    items += [("wo", 0), ("wo", 1), ("wo", 2), ("sgate", 0), ("sup", 0), ("sdown", 0)]
    slots += [0, 1, 2, 0, 1, 2]
    return items, slots


def build(nc, a, out):
    (y_p, y_s, kp0, vp0, kp1, vp1, kp2, vp2, conv_p, ks0, vs0, ks1, vs1, ks2, vs2, conv_s) = out
    k_prompt, v_prompt, k_sample, v_sample = (kp0, kp1, kp2), (vp0, vp1, vp2), (ks0, ks1, ks2), (vs0, vs1, vs2)
    k_cache = (a["cache_k_w128"], a["cache_k_w512"], a["cache_k_w2048"])
    v_cache = (a["cache_v_w128"], a["cache_v_w512"], a["cache_v_w2048"])
    mods_d = nc.dram_tensor("mods_d", [1 + B, SEC], F32, kind="Internal").ap()
    new_d = nc.dram_tensor("new_d", [3, NS, AW], F32, kind="Internal").ap()
    bias_d = nc.dram_tensor("bias_d", [G * H, NVEC * VL], F32, kind="Internal").ap()
    h2_d = nc.dram_tensor("h2_d", [TR, HROW], F32, kind="Internal").ap()
    y_d = nc.dram_tensor("y_d", [TR, D], F32, kind="Internal").ap()

    w_ada = a["w_ada"].rearrange("z (k p) n -> p (z k) n", p=P)
    w_in = a["w_in"].rearrange("z (k p) n -> p (z k) n", p=P)
    w_o = a["w_o"].rearrange("z (k p) n -> p (z k) n", p=P)
    xp = a["x_prompt"].rearrange("z (l r) d -> (z r) l d", r=DIL)
    xs = a["x_sample"].rearrange("b t d -> (b t) d")
    yp = y_p.rearrange("z (l r) d -> (z r) l d", r=DIL)
    ys = y_s.rearrange("b t d -> (b t) d")

    with ExitStack() as ctx:
        mem = ctx.enter_context(nc.sbuf_tensor("mem", [P, 53100], F32))
        top = [0]

        def take(n):
            top[0] += n
            assert top[0] <= 53100, top[0]
            return top[0] - n

        def at(off, *dims, parts=P):
            n = int(np.prod(dims))
            v = mem[0:parts, off:off + n]
            if len(dims) == 2:
                v = v.rearrange("p (a b) -> p a b", a=dims[0])
            elif len(dims) == 3:
                v = v.rearrange("p (a b c) -> p a b c", a=dims[0], b=dims[1])
            return v

        def tensor(*dims, parts=P):
            return at(take(int(np.prod(dims))), *dims, parts=parts)

        def sem(name):
            return ctx.enter_context(nc.semaphore(name))

        m_ring = take(RING * SLOT)
        m_hT = take(KD * NTOK)
        m_qk = take(2 * 6 * NTOK)
        m_vr = take(TILES * AW)
        m_kn = take(5 * PJ_W)
        m_mod = take(4 * D)
        m_smp = take(7 * D)
        m_att = take(3072)
        m_cv = take(3204)
        ring = [at(m_ring + SLOT * i, SLOT) for i in range(RING)]
        ring += [at(m_hT, SLOT), at(m_qk + NVEC * VL, SLOT), at(m_cv, SLOT)]
        x_t = tensor(TILES, D)
        hT = at(m_hT, KD, NTOK)
        catT = at(m_hT, KD, NTOK)
        qT, kT = at(m_qk, 6, NTOK), at(m_qk + 6 * NTOK, 6, NTOK)
        h2T = at(m_qk, KD, NTOK)
        hs = at(m_qk + KD * NTOK, 2, NTOK)
        v_r = at(m_vr, TILES, AW)
        kn = [at(m_kn + PJ_W * i, PJ_W) for i in range(3)]
        sq = [at(m_kn + PJ_W * (3 + i), PJ_W) for i in range(2)]
        wt = [at(m_kn + PJ_W * i, PJ_W) for i in range(2)]
        m1 = [[at(m_mod + D * (2 * s + i), D) for i in range(2)] for s in range(2)]
        tb = [at(m_mod + NVEC * P * i, NVEC, P) for i in range(2)]
        vm = at(m_mod + 2 * NVEC * P, GW + B * 2 * T)
        headmask, fold = vm[:, 0:GW], vm[:, GW:].rearrange("p (b s t) -> p b s t", b=B, s=2)
        vmul = [at(m_mod + 2 * NVEC * P + GW + B * 2 * T + GW * i, GW) for i in range(2)]
        part = at(m_mod + 3200, PJ_W, parts=NS)
        ohp, ohs = at(m_smp, NVEC * VL, parts=33), at(m_smp + NVEC * VL, T * SW, parts=32)
        sel = at(m_smp + NVEC * VL + T * SW, G, T, P, parts=G * H)
        k_buf = [at(m_smp + D * i, D) for i in range(KB)]
        q_buf = [at(m_smp + D * (KB + i), D) for i in range(KB)]
        prod = at(m_smp + D * 2 * KB, D)
        v_buf = [at(m_smp + D * i, D) for i in range(VB)]
        m2 = [[at(m_smp + D * (3 * s + i), D) for i in range(3)] for s in range(2)]
        h_row = [at(m_att + D * i, D) for i in range(2)]
        junk = at(m_att + 2 * D, D)
        crow = at(m_att, D, parts=1 + B)
        csig = at(m_att + D, D, parts=1 + B)
        sc_t = [at(m_att + 768 * i, 768) for i in range(2)]
        pT_t = [at(m_att + 768 * (2 + i), 768) for i in range(2)]
        bv = at(m_qk, NVEC * VL, parts=G * H)
        bs = at(m_cv, T * SW, parts=G * H)
        upP = at(m_cv, 2, 2 + SEQ)
        uT = at(m_cv + 2 * (2 + SEQ), 2, NTOK)
        gT = at(m_cv + 2 * (2 + SEQ) + 2 * NTOK, 2, NTOK)
        cst = tensor(CSTW)

        def const(name, parts=P, w=None):
            o, width = CST[name]
            return cst[0:parts, o:o + (w or width)]
        cT = tensor(KD * (1 + B))
        mrow = tensor(4, ADA_W, parts=1 + B)
        relb = tensor(G * H, parts=33)
        gq = tensor(DH)
        gk = tensor(DH)
        rows19 = at(m_vr + P, CC, parts=19)
        t19 = tensor(2, 19)
        upS = tensor(2, B, 2 + T)
        csx = tensor(2, 18)
        cso = at(m_att + 2 * D, CC, parts=18)
        st = tensor(G, P)
        stn = at(m_kn + 4 * PJ_W, G, P, parts=NS)
        ts = tensor(SW)
        sp = tensor(SW)
        spT = at(m_kn + 2 * PJ_W, 2 * G, P)
        wr = at(m_smp + 6 * D, KD, NE)
        br = tensor(NE)
        small = tensor(96)
        ss1, rs1, ss2, rs2 = (small[:, 8 * i:8 * i + TILES] for i in range(4))
        ssq = [small[:, 32 + 8 * i:38 + 8 * i] for i in range(2)]
        nmx, zs, rz = (small[:, 48 + 4 * i:50 + 4 * i] for i in range(3))
        snm, szs, srz = (small[:, 60 + i:61 + i] for i in range(3))

        h2_row = h_row
        sg = at(m_cv, 2, NTOK)
        y_row = [at(m_cv + 2 * NTOK + D * i, D) for i in range(2)]
        RW = TILES * NE
        r_sc, r_sel, r_ma, r_mr, r_m, r_g, r_pos, r_t8, r_gt, r_eq = (at(m_vr + RW * i, RW) for i in range(10))
        m_r = m_vr + 10 * RW
        r_gs, r_rank, r_gmb = (at(m_r + 40 * i, 40) for i in range(3))
        r_den = at(m_r + 120, TILES)
        r_cnt, r_nt, r_incl, r_base, r_cmp = (at(m_r + 128 + NE * i, NE) for i in range(5))
        r_top = at(m_r + 128 + 5 * NE, TILES, 8)
        zero = at(m_mod, HROW)
        g2 = [at(m_kn, D), at(m_att + 2 * D, D)]
        xg = [at(m_mod + HROW * i, HROW) for i in range(ET)]
        xT = [at(m_att + D * i, KD, P) for i in range(ET)]
        yo = [at(m_cv + D * i, D) for i in range(ET)]
        sge = [at(m_cv + 2 * D + FE * i, 2, P) for i in range(ET)]
        he = [at(m_cv + 2 * D + 2 * FE + FE * i, 2, P) for i in range(ET)]
        oneh = [at(m_kn + D + RW * i, RW).bitcast(BF16).rearrange("p (k n) -> p k n", k=TILES) for i in range(ET)]
        m_gu, m_dn = (m_hT, m_smp), (m_ring, m_smp + 4 * D)
        wgu = [at(m, 2, KD, FE) for m in m_gu]
        wdn = [at(m, 2, D) for m in m_dn]
        yf = [at(m_ring + D * i, D) for i in range(TILES)]
        meta = tensor(P + 8, parts=1).bitcast(I32)
        ecol = tensor(1)
        fcnt = tensor(1, parts=1)
        fpair = r_t8[0:1, 0:P]
        slotb = tensor(8).bitcast(BF16)
        ix = [tensor(1).bitcast(I32) for _ in range(ET)]
        ixs = [tensor(1).bitcast(I32) for _ in range(ET)]
        imt = tensor(3)
        gcol = [tensor(1) for _ in range(ET)]

        pb = [ctx.enter_context(nc.psum_tensor(f"pb{i}", [P, 512], F32)) for i in range(8)]

        s_cst, s_tables, s_in, s_x = sem("s_cst"), sem("s_tables"), sem("s_in"), sem("s_x")
        s_ring = [sem(f"s_ring{i}") for i in range(2 * RING)]
        s_set, s_csig, s_cs = sem("s_set"), sem("s_csig"), sem("s_cs")
        s_cT, s_smallT = sem("s_cT"), sem("s_smallT")
        s_bmm, s_bev, s_bvw, s_tsmm, s_ts = sem("s_bmm"), sem("s_bev"), sem("s_bvw"), sem("s_tsmm"), sem("s_ts")
        s_ada, s_mrow, s_each = sem("s_ada"), sem("s_mrow"), sem("s_each")
        s_modw = [sem(f"s_modw{i}") for i in range(4)]
        s_g1 = sem("s_g1")
        s_m1, s_m2, s_wr = sem("s_m1"), sem("s_m2"), sem("s_wr")
        s_ss1, s_var1, s_sd1 = sem("s_ss1"), sem("s_var1"), sem("s_sd1")
        s_h, s_hTp, s_hT = sem("s_h"), sem("s_hTp"), sem("s_hT")
        s_pj, s_sq, s_var, s_sd, s_pjq, s_kn, s_pjv, s_cmul = (sem(n) for n in (
            "s_pj", "s_sq", "s_var", "s_sd", "s_pjq", "s_kn", "s_pjv", "s_cmul"))
        s_part = sem("s_part")
        s_qkp, s_qk = sem("s_qkp"), sem("s_qk")
        s_kout = [sem(f"s_kout{i}") for i in range(3)]
        s_qout, s_vout, s_cout = sem("s_qout"), sem("s_vout"), sem("s_cout")
        s_link = sem("s_link")
        s_kq = [sem(f"s_kq{i}") for i in range(KB)]
        s_vb = [sem(f"s_vb{i}") for i in range(VB)]
        s_sco, s_snew, s_snT, s_sS, s_smx, s_sex, s_sP, s_sPTp, s_sPT, s_spv, s_sO = (sem(n) for n in (
            "s_sco", "s_snew", "s_snT", "s_sS", "s_smx", "s_sex", "s_sP", "s_sPTp", "s_sPT", "s_spv", "s_sO"))
        s_csx, s_csT, s_cso, s_conv = sem("s_csx"), sem("s_csT"), sem("s_cso"), sem("s_conv")
        s_tb = [sem(f"s_tb{i}") for i in range(2)]
        s_S, s_add, s_mx, s_ex, s_P, s_Tp, s_T, s_O, s_Oe = (sem(n) for n in (
            "s_S", "s_add", "s_mx", "s_ex", "s_P", "s_Tp", "s_T", "s_O", "s_Oe"))
        s_wo, s_wg, s_x1 = sem("s_wo"), sem("s_wg"), sem("s_x1")
        s_caches, s_newrows = sem("s_caches"), sem("s_newrows")
        s_vm, s_mask, s_fold = sem("s_vm"), sem("s_mask"), sem("s_fold")

        s_ss2, s_var2, s_sd2, s_h2, s_h2p, s_h2T = (sem(n) for n in (
            "s_ss2", "s_var2", "s_sd2", "s_h2", "s_h2p", "s_h2T"))
        s_h2w = [sem(f"s_h2w{i}") for i in range(2)]
        s_yw = [sem(f"s_yw{i}") for i in range(2)]
        s_lg, s_rz, s_sc, s_su, s_sg, s_hs, s_sd_, s_ysh, s_M, s_G, s_gw, s_rank, s_ecol, s_eT, s_meta = (
            sem(n) for n in ("s_lg", "s_rz", "s_sc", "s_su", "s_sg", "s_hs", "s_sd_", "s_ysh", "s_M", "s_G", "s_gw",
                             "s_rank", "s_ecol", "s_eT", "s_meta"))
        s_zw, s_g2 = sem("s_zw"), sem("s_g2")
        s_oneh, s_im, s_ix, s_tp, s_xa, s_xd, s_gc, s_upg, s_up, s_si, s_he, s_dn, s_ya, s_yd, s_ixs, s_sca = (
            sem(n) for n in ("s_oneh", "s_im", "s_ix", "s_tp", "s_xa", "s_xd", "s_gc", "s_upg", "s_up", "s_si", "s_he",
                             "s_dn", "s_ya", "s_yd", "s_ixs", "s_sca"))
        s_ga = [sem(f"s_ga{i}") for i in range(ET)]
        s_wgu = [sem(f"s_wgu{i}") for i in range(ET)]
        s_wdn = [sem(f"s_wdn{i}") for i in range(ET)]
        s_lrow, s_all, s_yf, s_fin, s_yout = sem("s_lrow"), sem("s_all"), [sem(f"s_yf{i}") for i in range(TILES)], sem("s_fin"), sem("s_yout")

        block = ctx.enter_context(nc.Block())
        items, slots_of = ring_items()

        def scale_of(i):
            return {1: "norm1_g", 4: "norm2_g"}.get(ADA_W * i // D)

        def previous_in_slot(n):
            same = [m for m in range(n) if slots_of[m] == slots_of[n]]
            return same[-1] if same else None

        landed = []
        for n, (kind, i) in enumerate(items):
            dmas = 1 if kind != "ada" else 3 if scale_of(i) else 2
            before = previous_in_slot(n)
            landed.append((0 if before is None else landed[before]) + 16 * dmas)


        def ada_row(n, q):
            return ring[slots_of[n]][0:1 + B, KD * ADA_W + ADA_W * q:KD * ADA_W + ADA_W * (q + 1)]

        copies = []
        for caches, dsts in ((k_cache, k_sample), (v_cache, v_sample)):
            for g in range(G):
                per = (B, 2, 1)[g]
                for b in range(0, B, per):
                    copies.append((dsts[g][0, b:b + per].rearrange("b w h d -> b (w h d)")[:, 0:(WB[g] - T) * GW],
                                   caches[g][0, b:b + per].rearrange("b w h d -> b (w h d)")[:, T * GW:]))

        def ring_uses(kind, i):
            return items.index((kind, i))

        def ada_after(c):
            return (1, 3) if c < 6 else (0, 1)

        def tok(j):
            return slice(P * j, P * j + (NS if j == SAMPLE else P))

        def nt(j):
            return NS if j == SAMPLE else P

        def sc_row(n):
            return n // B, n % B

        def evac_count(z):
            return (s_pjq, z + 1) if z < 20 else (s_pjv, z - 19) if z < 34 else (s_cmul, z - 33)

        @block.sync
        def _(eng):
            eng.dma_start(cst[:], a["k_cst"]).then_inc(s_cst, 16)
            eng.dma_start(crow[0:1, :], a["c_prompt"]).then_inc(s_in, 16)
            eng.dma_start(crow[1:1 + B, :], a["c_sample"]).then_inc(s_in, 16)
            eng.dma_start(rows19[0:16, :], a["state_conv"].rearrange("z b j c -> (z b j) c")).then_inc(s_in, 16)
            eng.dma_start(rows19[16:19, :], a["conv_w"].rearrange("z j c -> (z j) c")).then_inc(s_in, 16)
            for n, (kind, i) in enumerate(items):
                if previous_in_slot(n) is not None:
                    k0, i0 = items[previous_in_slot(n)]
                    if k0 == "ada":
                        eng.wait_ge(s_mrow, i0 + 1)
                    elif k0 == "proj":
                        eng.wait_ge(s_pj, pj_done(5 * i0 + 4 if i0 < 6 else 32 + 3 * (i0 - 6)))
                    else:
                        eng.wait_ge(s_wo, wo_done(5 * i0 + 4))
                slot = ring[slots_of[n]]
                if kind == "ada":
                    dst = slot[:, 0:KD * ADA_W].rearrange("p (k n) -> p k n", k=KD)
                    src = w_ada[:, :, ADA_W * i:ADA_W * (i + 1)]
                    cols = [a["b_ada"][:, ADA_W * i:ADA_W * (i + 1)]]
                    if scale_of(i):
                        c0 = ADA_W * i % D
                        cols.append(a[scale_of(i)][:, c0:c0 + ADA_W])
                    for q, col in enumerate(cols):
                        eng.dma_start(ada_row(n, q), col.to_broadcast([1 + B, ADA_W])).then_inc(s_ring[slots_of[n]], 16)
                elif kind == "proj":
                    dst = slot.rearrange("p (k n) -> p k n", k=KD)
                    src = w_in[:, :, PJ_W * i:PJ_W * (i + 1)]
                elif kind == "wo":
                    dst = slot[:, 0:KD * WO_W[i]].rearrange("p (k n) -> p k n", k=KD)
                    src = w_o[:, :, sum(WO_W[:i]):sum(WO_W[:i + 1])]
                elif kind == "sdown":
                    dst = slot[:, 0:2 * D].rearrange("p (k n) -> p k n", k=2)
                    src = a["w_down_s"].rearrange("z (k p) n -> p (z k) n", p=P)
                else:
                    dst = slot[:, 0:KD * FE].rearrange("p (k n) -> p k n", k=KD)
                    src = a["w_gate_s" if kind == "sgate" else "w_up_s"].rearrange("z (k p) n -> p (z k) n", p=P)
                eng.dma_start(dst, src).then_inc(s_ring[slots_of[n]], 16)
                if n == 5:
                    for r in range(DIL):
                        eng.dma_start(x_t[:, r, :], xp[r]).then_inc(s_x, 16)
                    eng.dma_start(x_t[0:NS, SAMPLE, :], xs).then_inc(s_x, 16)
            for j, tt in enumerate(ORDER):
                eng.wait_ge(s_h2, j + 1)
                eng.dma_start(h2_d[tok(tt), 0:D], h2_row[j % 2][0:nt(tt), :]).then_inc(s_h2w[j % 2], 16)
            eng.wait_ge(s_G, 1)
            for tt in range(TILES):
                eng.dma_start(h2_d[tok(tt), D:HROW], r_g[0:nt(tt), NE * tt:NE * (tt + 1)]).then_inc(s_gw, 16)
            eng.wait_ge(s_meta, 1)
            groups = eng.value_load(meta[0:1, P:P + 1], min_val=1, max_val=P // ET - 1)

            def weights(s, e, i):
                eng.wait_ge(s_up, ET * i + s + 1)
                for q, name in ((0, "w_gate_e"), (1, "w_up_e")):
                    eng.dma_start(wgu[s][:, q], a[name][0, bass.ds(e, 1)].rearrange("e (k p) f -> p (e k) f", p=P)
                                  ).then_inc(s_wgu[s], 16)
                eng.wait_ge(s_dn, 2 * (ET * i + s + 1))
                eng.dma_start(wdn[s], a["w_down_e"][0, bass.ds(e, 1)].rearrange("e (k p) n -> p (e k) n", p=P)
                              ).then_inc(s_wdn[s], 16)
            eng.wait_ge(s_su, 4)
            for s in range(ET):
                if s:
                    eng.wait_ge(s_ysh, 2 * TILES - 2)
                weights(s, eng.value_load(meta[0:1, s:s + 1], min_val=0, max_val=NE - 1), 0)
            with eng.Fori(1, groups) as i:
                for s in range(ET):
                    weights(s, eng.value_load(meta[0:1, bass.ds(ET * i + s, 1)], min_val=0, max_val=NE - 1), i)
            for s in range(ET):
                eng.wait_ge(s_wdn[s], 16 * groups)
            eng.wait_ge(s_all, 1)
            for tt in ORDER:
                eng.dma_start(yf[tt][0:nt(tt), :], y_d[tok(tt), :]).then_inc(s_yf[tt], 16)
            for s in range(ET):
                eng.wait_ge(s_wgu[s], 32 * groups)
            for j, tt in enumerate(ORDER):
                eng.wait_ge(s_fin, j + 1)
                eng.dma_start(ys if tt == SAMPLE else yp[tt], yf[tt][0:nt(tt), :]).then_inc(s_yout, 16)
            eng.wait_ge(s_caches, 16 * len(copies))
            eng.wait_ge(s_newrows, 16 * 6)
            eng.wait_ge(s_yout, 16 * TILES)

        @block.gpsimd
        def _(eng):
            eng.memset(relb[:], 1.0).then_inc(s_set, 1)
            eng.dma_start(ohp[:], a["k_ohp"]).then_inc(s_tables, 16)
            eng.dma_start(ohs[:], a["k_ohs"]).then_inc(s_tables, 16)
            eng.dma_start(sel[:], a["k_sel"].rearrange("q (g t p) -> q g t p", g=G, t=T)).then_inc(s_tables, 16)
            eng.wait_ge(s_set, 1)
            eng.dma_start(relb[0:32, :], a["rel_bias"]).then_inc(s_tables, 16)
            eng.dma_start(gq[:], a["q_norm_g"].to_broadcast([P, DH])).then_inc(s_tables, 16)
            eng.dma_start(gk[:], a["k_norm_g"].to_broadcast([P, DH])).then_inc(s_tables, 16)
            eng.dma_start(br[:], a["b_router"].to_broadcast([P, NE])).then_inc(s_tables, 16)
            eng.wait_ge(s_bev, 5)
            eng.dma_start(bias_d, bv[:]).then_inc(s_bvw, 16)

            def mod_out(i):
                eng.wait_ge(s_mrow, i + 1)
                eng.dma_start(mods_d[:, ADA_W * i:ADA_W * (i + 1)], mrow[:, i % 4, :]).then_inc(s_modw[i % 4], 16)

            def bcast(dst, sec, sample):
                src = mods_d[1:1 + B, D * sec:D * (sec + 1)] if sample else mods_d[0:1, D * sec:D * (sec + 1)]
                if sample:
                    for t in range(T):
                        yield dst[t:NS:T, :], src
                else:
                    yield dst, src.to_broadcast([P, D])

            eng.wait_ge(s_ts, 1)
            for i in range(ADA_1, ADA_1 + 4):
                mod_out(i)
            eng.wait_ge(s_qout, 32)
            for n in range(G * B):
                g, b = sc_row(n)
                if n >= KB:
                    eng.wait_ge(s_sco, n - KB + 1)
                w = KEYS[g]
                rows = k_cache[g][0, b].rearrange("(l r) h d -> l (r h d)", r=DILS[g])
                eng.dma_start(k_buf[n % KB][0:w, 0:(GW if g == 0 else D)], rows[0:w, 0:(GW if g == 0 else D)]
                              ).then_inc(s_kq[n % KB], 16)
                qsrc = new_d[0, T * b:T * (b + 1), GW * g:GW * (g + 1)].unsqueeze(0).to_broadcast([w, T, GW])
                eng.dma_start(q_buf[n % KB][0:w, :].rearrange("p (t n) -> p t n", t=T), qsrc).then_inc(s_kq[n % KB], 16)
                if n % 5 == 2 and n > 2:
                    mod_out(ADA_1 + 4 + 2 * (n // 5 - 1))
                    mod_out(ADA_1 + 5 + 2 * (n // 5 - 1))
            for i in range(ADA_N - 4, ADA_N):
                mod_out(i)
            eng.wait_ge(s_bvw, 16)
            eng.wait_ge(s_h, TILES)

            eng.dma_start(vm, a["k_vm"]).then_inc(s_vm, 16)

            def bias_table(h):
                for g, v0, nv in ((0, 0, 7), (1, 7, 1), (2, 8, 1)):
                    src = bass.AP(tensor=bias_d.tensor, offset=((g * H + h) * NVEC + v0) * VL,
                                  ap=[[1, P], [VL, nv], [1, P]])
                    eng.dma_start(tb[h % 2][:, v0:v0 + nv, :], src).then_inc(s_tb[h % 2], 16)
            bias_table(0)
            bias_table(1)

            def values(n):
                g, b = VUNITS[n]
                if n >= VB:
                    eng.wait_ge(s_spv, SPV[n - VB])
                w = KEYS[g]
                rows = v_cache[g][0, b].rearrange("(l r) h d -> l (r h d)", r=DILS[g])
                eng.dma_start(v_buf[n % VB][0:w, 0:(GW if g == 0 else D)], rows[0:w, 0:(GW if g == 0 else D)]
                              ).then_inc(s_vb[n % VB], 16)
            eng.wait_ge(s_sco, G * B)
            for n in range(VB):
                values(n)
            eng.wait_ge(s_add, H)
            bias_table(2)
            for n in range(VB, 2 * VB):
                values(n)
            eng.wait_ge(s_add, 2 * H)
            bias_table(3)
            for n in range(2 * VB, G * B):
                values(n)
            eng.wait_ge(s_spv, SPV[-1])
            for i in range(4):
                eng.wait_ge(s_modw[i], 16 * ((ADA_N - ADA_1) // 4))
            for i, sec in ((0, 2), (1, 4), (2, 3)):
                for s in (1, 0):
                    for dst, src in bcast(m2[s][i], sec, s == 1):
                        eng.dma_start(dst, src).then_inc(s_m2 if i else s_g1, 16)
            eng.dma_start(wr[:], a["w_router"].rearrange("z (k p) e -> p (z k) e", p=P)).then_inc(s_wr, 16)
            eng.wait_ge(s_add, 16)
            eng.memset(zero[:], 0.0).then_inc(s_set, 1)
            eng.wait_ge(s_set, 2)
            eng.dma_start(h2_d[NTOK:TR, :], zero[:]).then_inc(s_zw, 16)
            eng.dma_start(y_d[NTOK:TR, :], zero[:, 0:D]).then_inc(s_sca, 16)
            eng.wait_ge(s_x1, 15)
            eng.wait_ge(s_ss2, TILES)
            for s in range(2):
                for dst, src in bcast(g2[s], 5, s == 1):
                    eng.dma_start(dst, src).then_inc(s_g2, 16)
            eng.wait_ge(s_zw, 16)
            for i in range(2):
                eng.wait_ge(s_h2w[i], 16 * (3 - i))
            eng.wait_ge(s_gw, 16 * TILES)
            eng.wait_ge(s_meta, 1)
            groups = eng.value_load(meta[0:1, P:P + 1], min_val=1, max_val=P // ET - 1)

            gathers, added = eng.alloc_register("gathers"), eng.alloc_register("added")
            eng.reg_mov(gathers, 1)
            eng.reg_mov(added, 16)

            def gather(s, t):
                eng.wait_ge(s_ix, gathers)
                eng.reg_add(gathers, gathers, 1)
                eng.wait_ge(s_meta, 1)
                eng.indirect_dma_start(out=xg[s][:], out_offset=None, in_=h2_d,
                                       in_offset=bass.IndirectOffsetOnAxis(ap=ix[s][:, 0:1], axis=0)
                                       ).then_inc(s_ga[s], 16)
            gather(0, 0)
            gather(1, 1)
            for i in range(2):
                eng.wait_ge(s_yw[i], 16 * (3 - i))
            with eng.Fori(0, groups) as i:
                for s in range(ET):
                    t = ET * i + s
                    eng.wait_ge(s_tp, 2 * t + 2)
                    eng.wait_ge(s_gc, t + 1)
                    gather(s, t + 2)
                    eng.wait_ge(s_ya, t + 2)
                    eng.wait_ge(s_yd, t + 2)
                    eng.wait_ge(s_ixs, t + 1)
                    eng.wait_ge(s_sca, added)
                    eng.reg_add(added, added, 16)
                    eng.wait_ge(s_meta, 1)
                    eng.indirect_dma_start(out=y_d, out_offset=bass.IndirectOffsetOnAxis(ap=ixs[s][:, 0:1], axis=0),
                                           in_=yo[s][:], in_offset=None, compute_op=ALU.add).then_inc(s_sca, 16)
            eng.wait_ge(s_sca, 16 * ET * groups + 16)
            for s in range(ET):
                eng.wait_ge(s_ga[s], 16 * (groups + 1))
            eng.nop().then_inc(s_all, 1)

        @block.scalar
        def _(eng):
            eng.wait_ge(s_in, 16 * 4)
            eng.activation(csig[:], crow[:], ACT.Sigmoid).then_inc(s_csig, 1)
            eng.wait_ge(s_cT, 2)
            eng.activation(cT[:], pb[6][:, 0:72], ACT.Copy).then_inc(s_smallT, 1)
            eng.activation(t19[:].rearrange("p a b -> p (a b)"), pb[6][:, 192:230], ACT.Copy).then_inc(s_smallT, 1)
            for i in range(ADA_1):
                half, c0 = 1 - ADA_W * i // D, ADA_W * i % D
                eng.wait_ge(s_each, i + 1)
                eng.activation(m1[0][half][:, c0:c0 + ADA_W], pb[6 + i % 2][:, 0:ADA_W], ACT.Copy)
                eng.activation(m1[1][half][0:NS, c0:c0 + ADA_W], pb[6 + i % 2][0:NS, ADA_W:2 * ADA_W],
                               ACT.Copy).then_inc(s_m1, 1)
                j = i - 2
                if 0 <= j < TILES:
                    if j:
                        eng.wait_ge(s_ss1, j)
                    else:
                        eng.wait_ge(s_x, 16 * TILES)
                        eng.wait_ge(s_var1, 1)
                    eng.activation(junk[0:nt(j), :], x_t[0:nt(j), j, :], ACT.Square,
                                   accum_out=ss1[0:nt(j), j:j + 1]).then_inc(s_ss1, 1)
            eng.wait_ge(s_var1, 2)
            eng.activation(rs1, ss1, ACT.Sqrt).then_inc(s_sd1, 1)
            for q in range(9):
                c0 = 32 * (q % 4)
                eng.wait_ge(s_bmm, q + 1)
                if q < 5:
                    w = 512 if q < 4 else 256
                    eng.activation(bv[:, 512 * q:512 * q + w], pb[q % 4][c0:c0 + G * H, 0:w], ACT.Copy).then_inc(s_bev, 1)
                else:
                    eng.activation(bs[:, SW * (q - 5):SW * (q - 4)], pb[q % 4][c0:c0 + G * H, 0:SW],
                                   ACT.Copy).then_inc(s_bev, 1)
            for copy in copies[0:FIRST_COPIES]:
                eng.dma_start(*copy).then_inc(s_caches, 16)
            for j, tt in enumerate(ORDER):
                for half in range(2):
                    eng.wait_ge(s_hTp, 2 * j + half + 1)
                    n = nt(tt)
                    eng.activation(hT[:, 4 * half:4 * half + 4, tok(tt)],
                                   pb[2 + half][:, 0:4 * n].rearrange("p (k n) -> p k n", k=4),
                                   ACT.Copy).then_inc(s_hT, 1)

            def qk_out(z):
                c, tt = z // 5, ORDER[z % 5]
                n = nt(tt)
                eng.wait_ge(s_qkp, z + 1)
                dst = (qT, kT)[c // 2][:, 3 * (c % 2):3 * (c % 2) + 3, tok(tt)]
                eng.activation(dst, pb[2 + z % 2][:, 0:3 * n].rearrange("p (k n) -> p k n", k=3),
                               ACT.Copy).then_inc(s_qk, 1)
                if tt == SAMPLE:
                    eng.dma_start(new_d[c // 2, :, PJ_W * (c % 2):PJ_W * (c % 2 + 1)], kn[z % 3][0:NS, :]
                                  ).then_inc(s_qout if c < 2 else s_kout[z % 3], 16)
                elif c >= 2:
                    for g, lo, hi in KSEG[c % 2]:
                        skip = max(0, SEQ - WB[g]) // DIL
                        base = PJ_W * (c % 2) - GW * g
                        dst = k_prompt[g].rearrange("z y (l r) h d -> (z y r) l (h d)", r=DIL)[tt]
                        eng.dma_start(dst[:, base + lo:base + hi], kn[z % 3][skip:P, lo:hi]
                                      ).then_inc(s_kout[z % 3], 16)

            for c in range(8):
                for j, tt in enumerate(ORDER if c < 6 else range(3)):
                    n = nt(tt)
                    z = 5 * c + j if c < 6 else 30 + 3 * (c - 6) + j
                    whole = pb[z % 2][0:n, 0:PJ_W]
                    if z < 30 and tt == SAMPLE:
                        eng.wait_ge(s_part, c + 1)
                        whole = part
                    if z < 20:
                        eng.wait_ge(s_pj, pj_done(z))
                        if z >= 2:
                            eng.wait_ge(s_var, z - 1)
                        eng.activation(sq[z % 2][0:n, :], whole, ACT.Square).then_inc(s_sq, 1)
                        eng.wait_ge(s_var, z + 1)
                        eng.activation(ssq[z % 2][0:n, :], ssq[z % 2][0:n, :], ACT.Sqrt).then_inc(s_sd, 1)
                    elif z < 30:
                        eng.wait_ge(s_pj, pj_done(z))
                        eng.activation(v_r[0:n, tt, PJ_W * (c - 4):PJ_W * (c - 3)], whole,
                                       ACT.Copy).then_inc(s_pjv, 1)
                    elif z < 34:
                        eng.wait_ge(s_pj, pj_done(z))
                        dst = (uT, gT)[(z - 30) // 2][:, z % 2, :]
                        eng.activation(dst[:, 0:SEQ], pb[z % 2][:, :], ACT.Copy)
                        eng.activation(dst[:, SEQ:NTOK], pb[2 + z % 2][:, 0:NS], ACT.Copy).then_inc(s_pjv, 1)
                    if 1 <= z <= 20:
                        if z == 1:
                            eng.wait_ge(s_bvw, 16)
                        qk_out(z - 1)
                    if z in COPY_UNITS:
                        eng.dma_start(*copies[FIRST_COPIES + COPY_UNITS.index(z)]).then_inc(s_caches, 16)
            eng.wait_ge(s_pjv, 10)
            for r in range(DIL):
                for g in range(G):
                    skip = max(0, SEQ - WB[g]) // DIL
                    dst = v_prompt[g].rearrange("z y (l r) h d -> (z y r) l (h d)", r=DIL)[r]
                    eng.dma_start(dst, v_r[skip:P, r, GW * g:GW * (g + 1)]).then_inc(s_vout, 16)
            eng.dma_start(new_d[2], v_r[0:NS, SAMPLE, :]).then_inc(s_vout, 16)
            copied = FIRST_COPIES + len(COPY_UNITS)
            eng.wait_ge(s_snew, 1)
            for o in range(2):
                eng.activation(stn[:].rearrange("p g (e o n) -> p o g e n", e=2, o=2)[:, o],
                               pb[6 + o][0:NS, 0:2 * NS * G].rearrange("p (g e n) -> p g e n", g=G, e=2),
                               ACT.Copy).then_inc(s_snT, 1)
            eng.wait_ge(s_csT, 1)
            eng.activation(cso[:], pb[5][0:18, 0:CC], ACT.Copy).then_inc(s_cso, 1)
            eng.wait_ge(s_cso, 1)
            eng.dma_start(conv_p.rearrange("z y j c -> (z y j) c"), cso[0:2, :]).then_inc(s_cout, 16)
            eng.dma_start(conv_s.rearrange("z b j c -> (z b j) c"), cso[2:18, :]).then_inc(s_cout, 16)
            eng.wait_ge(s_smx, 1)
            eng.activation(sp[:], sp[:], ACT.Exp, bias=snm, accum_out=szs).then_inc(s_sex, 1)
            for u in range(18):
                if u in COPY_STEPS:
                    eng.dma_start(*copies[copied + COPY_STEPS.index(u)]).then_inc(s_caches, 16)
                if u < 16:
                    eng.wait_ge(s_mx, u + 1)
                    i = u % 2
                    eng.activation(sc_t[i][:], sc_t[i][:], ACT.Exp, bias=nmx[:, i:i + 1],
                                   accum_out=zs[:, i:i + 1]).then_inc(s_ex, 1)
                if u >= 2:
                    h, r = (u - 2) // 4, (u - 2) % 4
                    hb = DH * (h % 2)
                    eng.wait_ge(s_O, u - 1)
                    eng.activation(catT[hb:hb + DH, 0:6, P * r:P * (r + 1)].rearrange("p (g e) n -> p e g n", e=2)[:, h // 2],
                                   pb[6][hb:hb + DH, 0:G * P].rearrange("p (g n) -> p g n", g=G),
                                   ACT.Copy).then_inc(s_Oe, 1)
                if u == 1:
                    eng.wait_ge(s_sPTp, 1)
                    eng.activation(spT[:, 0:2, :], pb[7][:, 0:256].rearrange("p (a b) -> p a b", a=2), ACT.Copy)
                    eng.activation(spT[0:64, 2, :], pb[7][0:64, 256:384], ACT.Copy).then_inc(s_sPT, 1)
                if u == 2:
                    eng.wait_ge(s_sPTp, 2)
                    eng.activation(spT[0:NS, 3:6, :], pb[7][0:NS, 0:384].rearrange("p (a b) -> p a b", a=3),
                                   ACT.Copy).then_inc(s_sPT, 1)
                if 1 <= u <= 16:
                    i = (u - 1) % 2
                    if u == 1:
                        eng.wait_ge(s_cout, 32)
                    eng.wait_ge(s_Tp, 2 * u - 1)
                    if u >= 3:
                        eng.wait_ge(s_O, u - 2)
                    eng.activation(pT_t[i][:, 0:512], pb[4][:, :], ACT.Copy).then_inc(s_T, 1)
                    eng.wait_ge(s_Tp, 2 * u)
                    eng.activation(pT_t[i][:, 512:768], pb[5][:, 0:256], ACT.Copy).then_inc(s_T, 1)
            eng.wait_ge(s_fold, len(WIDE))
            for hh in range(2):
                o = pb[7][DH * hh:DH * (hh + 1), 0:384].rearrange("p (q s n) -> p s q n", q=6, s=2)[:, hh]
                eng.activation(catT[DH * hh:DH * (hh + 1), 0:6, SEQ:NTOK], o, ACT.Copy).then_inc(s_sO, 1)
            for i in range(3):
                eng.wait_ge(s_kout[i], KOUT[i])
            eng.wait_ge(s_vout, 16 * (DIL * G + 1))
            for kv, dsts in ((1, k_sample), (2, v_sample)):
                for g in range(G):
                    eng.dma_start(dsts[g][0, :, WB[g] - T:, :, :].rearrange("b t h d -> b t (h d)"),
                                  new_d[kv].rearrange("(b t) n -> b t n", t=T)[:, :, GW * g:GW * (g + 1)]
                                  ).then_inc(s_newrows, 16)
            for copy in copies[copied + len(COPY_STEPS):]:
                eng.dma_start(*copy).then_inc(s_caches, 16)
            for j, tt in enumerate(ORDER):
                eng.wait_ge(s_x1, 10 + j + 1)
                if j:
                    eng.wait_ge(s_ss2, j)
                eng.activation(junk[0:nt(tt), :], x_t[0:nt(tt), tt, :], ACT.Square,
                               accum_out=ss2[0:nt(tt), tt:tt + 1]).then_inc(s_ss2, 1)
                eng.wait_ge(s_var2, j + 1)
                eng.activation(rs2[0:nt(tt), tt:tt + 1], ss2[0:nt(tt), tt:tt + 1], ACT.Sqrt).then_inc(s_sd2, 1)
            eng.wait_ge(s_rz, 1)

            def sigmoid(j):
                tt = ORDER[j]
                eng.wait_ge(s_lg, j + 1)
                eng.activation(r_sc[0:nt(tt), NE * tt:NE * (tt + 1)], pb[4 + j % 2][0:nt(tt), 0:NE], ACT.Sigmoid
                               ).then_inc(s_sc, 1)
            for j, tt in enumerate(ORDER):
                n = nt(tt)
                for half in range(2):
                    eng.wait_ge(s_h2p, 2 * j + half + 1)
                    eng.activation(h2T[:, 4 * half:4 * half + 4, tok(tt)],
                                   pb[2 + half][:, 0:4 * n].rearrange("p (k n) -> p k n", k=4),
                                   ACT.Copy).then_inc(s_h2T, 1)
                if j:
                    sigmoid(j - 1)
            sigmoid(TILES - 1)
            for f in range(2):
                eng.wait_ge(s_su, 2 * f + 1)
                eng.activation(sg[:, f, 0:SEQ], pb[4 * f][:, :], ACT.Silu)
                eng.activation(sg[:, f, SEQ:NTOK], pb[4 * f + 2][:, 0:NS], ACT.Silu).then_inc(s_sg, 1)
            for j, tt in enumerate(ORDER):
                if j >= 2:
                    eng.wait_ge(s_yw[j % 2], 16 * (j // 2))
                for half in range(2):
                    u = 2 * j + half
                    eng.wait_ge(s_sd_, u + 1)
                    eng.activation(y_row[j % 2][0:nt(tt), 512 * half:512 * half + 512], pb[YB[u % 4]][0:nt(tt), :],
                                   ACT.Copy).then_inc(s_ysh, 1)
                eng.wait_ge(s_ysh, 2 * j + 2)
                eng.dma_start(y_d[tok(tt), :], y_row[j % 2][0:nt(tt), :]).then_inc(s_yw[j % 2], 16)
            eng.wait_ge(s_meta, 1)
            groups = eng.value_load(meta[0:1, P:P + 1], min_val=1, max_val=P // ET - 1)

            def x_evac(s, t):
                eng.wait_ge(s_tp, 2 * t + 1)
                eng.activation(xT[s][:, 0:4, :], pb[4][:, :].rearrange("p (k n) -> p k n", k=4), ACT.Copy
                               ).then_inc(s_xa, 1)
            x_evac(0, 0)
            eng.nop().then_inc(s_ya, 1)
            for i in range(2):
                eng.wait_ge(s_yw[i], 16 * (3 - i))
            with eng.Fori(0, groups) as i:
                for s in range(ET):
                    t = ET * i + s
                    eng.wait_ge(s_upg, t + 1)
                    eng.wait_ge(s_he, t + 1)
                    eng.activation(sge[s], pb[0][:, 0:2 * P].rearrange("p (f n) -> p f n", f=2), ACT.Silu
                                   ).then_inc(s_si, 1)
                    x_evac(1 - s, t + 1)
                    eng.wait_ge(s_dn, 2 * ET + 2 * t + 1)
                    eng.wait_ge(s_gc, t + 1)
                    eng.wait_ge(s_ixs, t + 1)
                    eng.activation(yo[s][:, 0:512], pb[2][:, :], ACT.Copy, scale=gcol[s]).then_inc(s_ya, 1)

        @block.tensor
        def _(eng):
            ident, flip = const("ident"), const("flip")

            def turn(dst, src, parts):
                return eng.transpose(dst, src, ident[0:parts, 0:parts])

            def ring_in(n):
                eng.wait_ge(s_ring[slots_of[n]], landed[n])

            eng.wait_ge(s_cst, 16)
            eng.wait_ge(s_cs, 1)
            for k in range(KD):
                last = turn(pb[6][:, 9 * k:9 * k + 9], csig[:, P * k:P * (k + 1)], 9)
            last.then_inc(s_cT, 1)
            turn(pb[6][:, 192:211], rows19[:, 0:P], 19)
            turn(pb[6][:, 211:230], rows19[:, P:CC], 19).then_inc(s_cT, 1)

            def ada(i):
                n = ring_uses("ada", i)
                ring_in(n)
                w = ring[slots_of[n]][:, 0:KD * ADA_W].rearrange("p (k n) -> p k n", k=KD)
                if i >= 2:
                    eng.wait_ge(s_mrow, i - 1)
                for k in range(KD):
                    q = 32 * (k % 4)
                    mm = eng.matmul(pb[4 + i % 2][q:q + 1 + B, 0:ADA_W], lhsT=cT[:, 9 * k:9 * k + 9], rhs=w[:, k, :],
                                    start=(k < 4), stop=(k >= KD - 4))
                    if k >= KD - 4:
                        mm.then_inc(s_ada, 1)

            def to_tokens(i):
                eng.wait_ge(s_mrow, i + 1)
                if i >= 2:
                    eng.wait_ge(s_m1, i - 1)
                each = const("each", parts=1 + B)
                eng.matmul(pb[6 + i % 2][:, 0:ADA_W], lhsT=each[:, 0:P], rhs=mrow[:, i % 4, :], start=True, stop=True)
                eng.matmul(pb[6 + i % 2][0:NS, ADA_W:2 * ADA_W], lhsT=each[:, P:P + NS], rhs=mrow[:, i % 4, :],
                           start=True, stop=True).then_inc(s_each, 1)

            eng.wait_ge(s_smallT, 2)
            for i in range(ADA_1):
                ada(i)
                if i:
                    to_tokens(i - 1)
            to_tokens(ADA_1 - 1)
            eng.wait_ge(s_tables, 16 * 7)
            for q in range(9):
                if q >= 4:
                    eng.wait_ge(s_bev, q - 3)
                c0 = 32 * (q % 4)
                if q < 5:
                    w = 512 if q < 4 else 256
                    mm = eng.matmul(pb[q % 4][c0:c0 + G * H, 0:w], lhsT=relb[:], rhs=ohp[:, 512 * q:512 * q + w],
                                    start=True, stop=True)
                else:
                    mm = eng.matmul(pb[q % 4][c0:c0 + G * H, 0:SW], lhsT=relb[0:32, :], rhs=ohs[:, SW * (q - 5):SW * (q - 4)],
                                    start=True, stop=True)
                mm.then_inc(s_bmm, 1)
            eng.wait_ge(s_bev, 9)
            eng.wait_ge(s_m1, ADA_1)
            for g in range(G):
                for t in range(T):
                    c0 = SW * t + SOFF[g]
                    mm = eng.matmul(pb[7][:, SOFF[g]:SOFF[g] + SEG[g]], lhsT=sel[:, g, t, :], rhs=bs[:, c0:c0 + SEG[g]],
                                    start=(t == 0), stop=(t == T - 1))
            mm.then_inc(s_tsmm, 1)
            for j, tt in enumerate(ORDER):
                n = nt(tt)
                eng.wait_ge(s_h, j + 1)
                for k in range(KD):
                    if k % 4 == 0 and j:
                        eng.wait_ge(s_hT, 2 * j - 1 + k // 4)
                    mm = turn(pb[2 + k // 4][:, n * (k % 4):n * (k % 4 + 1)], h_row[j % 2][0:n, P * k:P * (k + 1)], n)
                    if k % 4 == 3:
                        mm.then_inc(s_hTp, 1)

            def quarters(bank, width, xT, w, done):
                for k in range(KD):
                    c0 = NS * (k % 4)
                    mm = eng.matmul(bank[c0:c0 + NS, 0:width], lhsT=xT[:, k, tok(SAMPLE)], rhs=w[:, k, :],
                                    start=(k < 4), stop=(k >= KD - 4))
                    if k >= KD - 4:
                        mm.then_inc(done, 1)

            def qk_turn(z):
                tt = ORDER[z % 5]
                n = nt(tt)
                eng.wait_ge(s_kn, z + 1)
                if z >= 2:
                    eng.wait_ge(s_qk, z - 1)
                for m in range(3):
                    to, rows = pb[2 + z % 2][:, n * m:n * (m + 1)], kn[z % 3][0:n, P * m:P * (m + 1)]
                    if z < 10 and tt != SAMPLE:
                        last = eng.matmul(to, lhsT=rows, rhs=flip, start=True, stop=True)
                    else:
                        last = turn(to, rows, n)
                last.then_inc(s_qkp, 1)

            eng.wait_ge(s_hT, 2 * TILES)
            for c in range(8):
                n = ring_uses("proj", c)
                ring_in(n)
                w = ring[slots_of[n]].rearrange("p (k n) -> p k n", k=KD)
                for j, tt in enumerate(ORDER if c < 6 else range(3)):
                    z = 5 * c + j if c < 6 else 30 + 3 * (c - 6) + j
                    if z >= 2:
                        eng.wait_ge(*evac_count(z - 2))
                    if c < 6 and tt == SAMPLE:
                        quarters(pb[z % 2], PJ_W, hT, w, s_pj)
                    elif c < 6:
                        for k in range(KD):
                            mm = eng.matmul(pb[z % 2][0:nt(tt), 0:PJ_W], lhsT=hT[:, k, tok(tt)], rhs=w[:, k, :],
                                            start=(k == 0), stop=(k == KD - 1))
                    else:
                        for k in range(KD):
                            eng.matmul(pb[z % 2][:, :], lhsT=w[:, k, P * j:P * (j + 1)], rhs=hT[:, k, 0:SEQ],
                                       start=(k == 0), stop=(k == KD - 1))
                        for k in range(KD):
                            mm = eng.matmul(pb[2 + z % 2][:, 0:NS], lhsT=w[:, k, P * j:P * (j + 1)],
                                            rhs=hT[:, k, SEQ:NTOK], start=(k == 0), stop=(k == KD - 1))
                    if c >= 6 or tt != SAMPLE:
                        mm.then_inc(s_pj, 1)
                    if 1 <= z <= 20:
                        qk_turn(z - 1)
                    if z == 29:
                        eng.wait_ge(s_qk, 20)
                    if j in ada_after(c):
                        ada(ADA_1 + 2 * c + ada_after(c).index(j))
            eng.wait_ge(s_mrow, ADA_N)
            for h in (0, 2, 1, 3):
                for g in range(G):
                    hb, q = DH * (h % 2), 2 * g + h // 2
                    c0 = 2 * NS * g + NS * (h // 2)
                    mm = eng.matmul(pb[6 + h % 2][0:NS, c0:c0 + NS], lhsT=kT[hb:hb + DH, q, SEQ:NTOK],
                                    rhs=qT[hb:hb + DH, q, SEQ:NTOK], start=True, stop=True)
            mm.then_inc(s_snew, 1)
            eng.wait_ge(s_csx, 2)
            eng.wait_ge(s_mrow, ADA_N)
            turn(pb[5][0:18, 0:P], csx[:, 0, :], P)
            turn(pb[5][0:18, P:CC], csx[:, 1, :], P).then_inc(s_csT, 1)
            eng.wait_ge(s_sco, G * B)
            eng.wait_ge(s_snT, 2)
            for g in range(G):
                turn(pb[7][:, SOFF[g]:SOFF[g] + KEYS[g]], st[0:KEYS[g], g, :], KEYS[g])
                last = turn(pb[7][:, SOFF[g] + KEYS[g]:SOFF[g] + SEG[g]], stn[:, g, :], NS)
            last.then_inc(s_sS, 1)
            eng.wait_ge(s_cmul, 2)
            eng.wait_ge(s_cso, 1)

            def wide_values(m):
                g, b = WIDE[m]
                n = VUNITS.index(WIDE[m])
                eng.wait_ge(s_vb[n % VB], 16 * (n // VB + 1))
                if m >= 2:
                    eng.wait_ge(s_mask, m - 1)
                for t in range(T):
                    pr = spT[0:KEYS[g], g, :].rearrange("p (x t) -> p t x", t=T)[:, t]
                    eng.matmul(pb[2 * (m % 2) + 1][NS * t:NS * (t + 1), GW:2 * GW], lhsT=pr,
                               rhs=v_buf[n % VB][0:KEYS[g], GW * t:GW * (t + 1)], start=True, stop=True
                               ).then_inc(s_spv, 1)

            def fold_values(m):
                g, b = WIDE[m]
                eng.wait_ge(s_mask, m + 1)
                for hp in range(2):
                    q = 2 * g + hp
                    o = pb[7][:, 64 * q:64 * (q + 1)].rearrange("p (s n) -> p s n", s=2)
                    mm = eng.matmul(o[:, :, T * b:T * (b + 1)], lhsT=vmul[m % 2][:, P * hp:P * (hp + 1)],
                                    rhs=fold[:, b], start=False, stop=(m == len(WIDE) - 1), skip_group_check=True)
                mm.then_inc(s_fold, 1)

            for u in range(18):
                if u >= 2:
                    eng.wait_ge(s_add, u - 1)
                    if u == 2:
                        eng.wait_ge(s_sPT, 1)
                    wide_values(u - 2)
                if u < 16:
                    h, r = u // 4, u % 4
                    hb, q = DH * (h % 2), h // 2
                    lo, hi = pb[2 * (u % 2)], pb[2 * (u % 2) + 1]
                    eng.matmul(lo[:, :], lhsT=qT[hb:hb + DH, q, tok(r)], rhs=kT[hb:hb + DH, q, 0:SEQ],
                               start=True, stop=True)
                    for g in (1, 2):
                        mm = eng.matmul(hi[:, P * (g - 1):P * g], lhsT=qT[hb:hb + DH, 2 * g + q, tok(r)],
                                        rhs=kT[hb:hb + DH, 2 * g + q, tok(r)], start=True, stop=True)
                    mm.then_inc(s_S, 1)
                if u >= 2:
                    h, r = (u - 2) // 4, (u - 2) % 4
                    hb, pt = DH * (h % 2), pT_t[u % 2]
                    eng.wait_ge(s_T, 2 * (u - 1))
                    if u >= 3:
                        eng.wait_ge(s_Oe, u - 2)
                    for rk in range(DIL):
                        eng.matmul(pb[6][hb:hb + DH, 0:P], lhsT=v_r[:, rk, DH * h:DH * (h + 1)],
                                   rhs=pt[:, P * rk:P * (rk + 1)], start=(rk == 0), stop=(rk == DIL - 1))
                    for g in (1, 2):
                        mm = eng.matmul(pb[6][hb:hb + DH, P * g:P * (g + 1)],
                                        lhsT=v_r[:, r, GW * g + DH * h:GW * g + DH * (h + 1)],
                                        rhs=pt[:, P * (3 + g):P * (4 + g)], start=True, stop=True)
                    mm.then_inc(s_O, 1)
                if u == 1:
                    eng.wait_ge(s_sP, 1)
                    for g in range(G):
                        last = turn(pb[7][0:KEYS[g], P * g:P * (g + 1)], sp[:, SOFF[g]:SOFF[g] + KEYS[g]], P)
                    last.then_inc(s_sPTp, 1)
                if u == 2:
                    eng.wait_ge(s_sPT, 1)
                    for g in range(G):
                        last = turn(pb[7][0:NS, P * g:P * (g + 1)], sp[:, SOFF[g] + KEYS[g]:SOFF[g] + SEG[g]], P)
                    last.then_inc(s_sPTp, 1)
                if u == 3:
                    eng.wait_ge(s_sPT, 2)
                    for g in range(G):
                        for hp in range(2):
                            q = 2 * g + hp
                            eng.matmul(pb[7][:, 64 * q:64 * (q + 1)], lhsT=v_r[0:NS, SAMPLE, P * q:P * (q + 1)],
                                       rhs=spT[0:NS, 3 + g, 64 * hp:64 * (hp + 1)], start=(q == 0), stop=False,
                                       skip_group_check=True)
                if 3 <= u < 3 + B:
                    b = u - 3
                    n = VUNITS.index((0, b))
                    eng.wait_ge(s_vb[n % VB], 16 * (n // VB + 1))
                    for hp in range(2):
                        o = pb[7][:, 64 * hp:64 * (hp + 1)].rearrange("p (s n) -> p s n", s=2)
                        pr = spT[0:KEYS[0], 0, 64 * hp:64 * (hp + 1)].rearrange("p (s n) -> p s n", s=2)
                        mm = eng.matmul(o[:, :, T * b:T * (b + 1)], lhsT=v_buf[n % VB][0:KEYS[0], P * hp:P * (hp + 1)],
                                        rhs=pr[:, :, T * b:T * (b + 1)], start=False, stop=False, skip_group_check=True)
                    mm.then_inc(s_spv, 1)
                if u >= 3:
                    fold_values(u - 3)
                if 1 <= u <= 16:
                    eng.wait_ge(s_P, u)
                    if u >= 2:
                        eng.wait_ge(s_T, 2 * (u - 1))
                    for m in range(6):
                        mm = eng.matmul((pb[4][:, P * m:P * (m + 1)] if m < 4 else pb[5][:, P * (m - 4):P * (m - 3)]),
                                        lhsT=sc_t[(u - 1) % 2][:, P * m:P * (m + 1)], rhs=flip, start=True, stop=True)
                        if m in (3, 5):
                            mm.then_inc(s_Tp, 1)
            fold_values(len(WIDE) - 1)
            eng.wait_ge(s_Oe, 16)
            eng.wait_ge(s_sO, 2)
            eng.wait_ge(s_conv, 4)
            eng.wait_ge(s_add, 16)
            for o in range(3):
                n = ring_uses("wo", o)
                ring_in(n)
                w = ring[slots_of[n]][:, 0:KD * WO_W[o]].rearrange("p (k n) -> p k n", k=KD)
                for j, tt in enumerate(ORDER):
                    u = 5 * o + j
                    if u >= 2:
                        eng.wait_ge(s_wg, u - 1)
                    if tt == SAMPLE:
                        quarters(pb[u % 2], WO_W[o], catT, w, s_wo)
                        continue
                    for k in range(KD):
                        mm = eng.matmul(pb[u % 2][0:nt(tt), 0:WO_W[o]], lhsT=catT[:, k, tok(tt)], rhs=w[:, k, :],
                                        start=(k == 0), stop=(k == KD - 1))
                    mm.then_inc(s_wo, 1)
            eng.wait_ge(s_wr, 16)

            def router(j):
                tt = ORDER[j]
                eng.wait_ge(s_h2T, 2 * j + 2)
                if j >= 2:
                    eng.wait_ge(s_sc, j - 1)
                for k in range(KD):
                    mm = eng.matmul(pb[4 + j % 2][0:nt(tt), 0:NE], lhsT=h2T[:, k, tok(tt)], rhs=wr[:, k, :],
                                    start=(k == 0), stop=(k == KD - 1))
                mm.then_inc(s_lg, 1)
            for j, tt in enumerate(ORDER):
                n = nt(tt)
                eng.wait_ge(s_h2, j + 1)
                for k in range(KD):
                    if k % 4 == 0 and j:
                        eng.wait_ge(s_h2T, 2 * j - 1 + k // 4)
                    mm = turn(pb[2 + k // 4][:, n * (k % 4):n * (k % 4 + 1)], h2_row[j % 2][0:n, P * k:P * (k + 1)], n)
                    if k % 4 == 3:
                        mm.then_inc(s_h2p, 1)
                if j:
                    router(j - 1)
            router(TILES - 1)
            n_g, n_u, n_d = (ring_uses(k, 0) for k in ("sgate", "sup", "sdown"))
            eng.wait_ge(s_wg, 15)
            eng.wait_ge(s_h2T, 2 * TILES)
            ring_in(n_g)
            ring_in(n_u)
            upper, ones = const("upper"), const("ones")

            def ranks():
                eng.wait_ge(s_M, 1)
                eng.wait_ge(s_hs, 1)
                for k in range(TILES):
                    for j in range(k + 1):
                        eng.matmul(pb[3][:, NE * k:NE * (k + 1)], lhsT=upper if j == k else ones,
                                   rhs=r_m[:, NE * j:NE * (j + 1)], start=(j == 0), stop=(j == k))
                for j in range(TILES):
                    mm = eng.matmul(pb[3][:, RW:RW + NE], lhsT=ones, rhs=r_m[:, NE * j:NE * (j + 1)],
                                    start=(j == 0), stop=(j == TILES - 1))
                mm.then_inc(s_rank, 1)

            for f in range(2):
                if f:
                    ranks()
                    eng.wait_ge(s_sc, TILES)
                for q, n in ((0, n_g), (1, n_u)):
                    if f and q:
                        eng.wait_ge(s_ecol, 1)
                        turn(pb[3][0:1, RW:RW + P], ecol[:], P).then_inc(s_eT, 1)
                    w = ring[slots_of[n]][:, 0:KD * FE].rearrange("p (k n) -> p k n", k=KD)
                    for k in range(KD):
                        eng.matmul(pb[4 * f + q][:, :], lhsT=w[:, k, P * f:P * (f + 1)], rhs=h2T[:, k, 0:SEQ],
                                   start=(k == 0), stop=(k == KD - 1))
                    for k in range(KD):
                        mm = eng.matmul(pb[4 * f + q + 2][:, 0:NS], lhsT=w[:, k, P * f:P * (f + 1)],
                                        rhs=h2T[:, k, SEQ:NTOK], start=(k == 0), stop=(k == KD - 1))
                    mm.then_inc(s_su, 1)
            for s in range(ET):
                eng.nop().then_inc(s_up, 1)
                eng.nop().then_inc(s_dn, 1)
                eng.nop().then_inc(s_dn, 1)
            ring_in(n_d)
            wd = ring[slots_of[n_d]][:, 0:2 * D].rearrange("p (k n) -> p k n", k=2)
            eng.wait_ge(s_hs, 2)

            def shared_down(u):
                tt, half = ORDER[u // 2], u % 2
                if u >= 4:
                    eng.wait_ge(s_ysh, u - 3)
                for f in range(2):
                    mm = eng.matmul(pb[YB[u % 4]][0:nt(tt), :], lhsT=hs[:, f, tok(tt)], rhs=wd[:, f, 512 * half:512 * half + 512],
                                    start=(f == 0), stop=(f == 1))
                mm.then_inc(s_sd_, 1)
            eng.wait_ge(s_meta, 1)
            groups = eng.value_load(meta[0:1, P:P + 1], min_val=1, max_val=P // ET - 1)

            def slots(s, t):
                eng.wait_ge(s_oneh, t + 1)
                for k in range(TILES):
                    mm = eng.matmul(pb[6][:, 0:3], lhsT=oneh[s][:, k, :], rhs=slotb[:, 3 * k:3 * k + 3],
                                    start=(k == 0), stop=(k == TILES - 1))
                mm.then_inc(s_im, 1)

            for u in range(10):
                shared_down(u)
                if u == 0:
                    slots(0, 0)
                if u == 2:
                    eng.wait_ge(s_ix, 1)
                    slots(1, 1)
            eng.wait_ge(s_ysh, 10)

            def x_turn(s, t, uses):
                eng.wait_ge(s_ga[s], 16 * uses)
                for k in range(KD):
                    mm = turn(pb[4 + k // 4][:, P * (k % 4):P * (k % 4 + 1)], xg[s][:, P * k:P * (k + 1)], P)
                    if k % 4 == 3:
                        mm.then_inc(s_tp, 1)
            x_turn(0, 0, 1)
            with eng.Fori(0, groups) as i:
                for s in range(ET):
                    t = ET * i + s
                    eng.wait_ge(s_wgu[s], 32 * i + 32)
                    eng.wait_ge(s_xa, t + 1)
                    eng.wait_ge(s_xd, t + 1)
                    for q in range(2):
                        for f in range(2):
                            for k in range(KD):
                                mm = eng.matmul(pb[q][:, P * f:P * (f + 1)], lhsT=wgu[s][:, q, k, P * f:P * (f + 1)],
                                                rhs=xT[s][:, k, :], start=(k == 0), stop=(k == KD - 1))
                        mm.then_inc((s_upg, s_up)[q], 1)
                    eng.wait_ge(s_ix, t + 2)
                    slots(s, t + 2)
                    x_turn(1 - s, t + 1, i + 1 + s)
                    eng.wait_ge(s_he, t + 2)
                    eng.wait_ge(s_wdn[s], 16 * i + 16)
                    eng.wait_ge(s_ya, t + 1)
                    eng.wait_ge(s_yd, t + 1)
                    for half in range(2):
                        for f in range(2):
                            mm = eng.matmul(pb[2 + half][:, :], lhsT=he[s][:, f, :],
                                            rhs=wdn[s][:, f, 512 * half:512 * half + 512], start=(f == 0), stop=(f == 1))
                        mm.then_inc(s_dn, 1)

        @block.vector
        def _(eng):
            links = [0]

            def link(ins):
                links[0] += 1
                ins.then_inc(s_link, 1)
                eng.wait_ge(s_link, links[0])

            link(eng.memset(ss1, 1.0))
            link(eng.memset(ss2, 1.0))
            eng.wait_ge(s_csig, 1)
            eng.tensor_tensor(csig[:], csig[:], crow[:], ALU.mult).then_inc(s_cs, 1)
            eng.nop().then_inc(s_var1, 1)
            eng.wait_ge(s_smallT, 2)
            for m in range(2):
                link(eng.tensor_copy(upS[:, m, :, 0:2], t19[:, m, 0:16].rearrange("p (b j) -> p b j", j=2)))
            def ada_evac(i):
                n = ring_uses("ada", i)
                eng.wait_ge(s_ada, 4 * (i + 1))
                if 4 <= i < ADA_1 + 4:
                    eng.wait_ge(s_each, i - 3)
                elif i >= 4:
                    eng.wait_ge(s_modw[i % 4], 16 * ((i - ADA_1) // 4))
                dst = mrow[:, i % 4, :]
                add = eng.tensor_tensor(dst, pb[4 + i % 2][0:1 + B, 0:ADA_W], ada_row(n, 0), ALU.add)
                for q in (32, 64, 96):
                    link(add)
                    add = eng.tensor_tensor(dst, pb[4 + i % 2][q:q + 1 + B, 0:ADA_W], dst, ALU.add)
                if scale_of(i):
                    link(add)
                    add = eng.scalar_tensor_tensor(out=dst, in0=dst, scalar=1.0, in1=ada_row(n, 1), op0=ALU.add,
                                                   op1=ALU.mult)
                add.then_inc(s_mrow, 1)

            for i in range(ADA_1):
                ada_evac(i)
            eng.wait_ge(s_tables, 16 * 7)
            link(eng.tensor_scalar(gq[:], gq[:], DH ** -0.5, None, ALU.mult))
            eng.wait_ge(s_ss1, TILES)
            eng.tensor_scalar(ss1, ss1, 1.0 / D, EPS, ALU.mult, ALU.add).then_inc(s_var1, 1)
            eng.wait_ge(s_sd1, 1)
            link(eng.reciprocal(rs1, rs1))
            eng.wait_ge(s_m1, ADA_1)
            for j, tt in enumerate(ORDER):
                n, s = nt(tt), int(tt == SAMPLE)
                if j == 2:
                    eng.wait_ge(s_tsmm, 1)
                    eng.tensor_tensor(ts[:], pb[7][:, 0:SW], const("smask"), ALU.add).then_inc(s_ts, 1)
                if j >= 2:
                    eng.wait_ge(s_hTp, 2 * j - 2)
                link(eng.scalar_tensor_tensor(out=h_row[j % 2][0:n, :], in0=x_t[0:n, tt, :], scalar=rs1[0:n, tt:tt + 1],
                                              in1=m1[s][0][0:n, :], op0=ALU.mult, op1=ALU.mult))
                eng.tensor_tensor(h_row[j % 2][0:n, :], h_row[j % 2][0:n, :], m1[s][1][0:n, :], ALU.add
                                  ).then_inc(s_h, 1)

            def score(n):
                g, b = sc_row(n)
                w = KEYS[g]
                eng.wait_ge(s_kq[n % KB], 32 * (n // KB + 1))
                if n:
                    eng.wait_ge(s_sco, n)
                kk = k_buf[n % KB][0:w, 0:GW].unsqueeze(1).to_broadcast([w, T, GW]) if g == 0 else \
                    k_buf[n % KB][0:w, :].rearrange("p (t n) -> p t n", t=T)
                link(eng.tensor_tensor(prod[0:w, :].rearrange("p (t n) -> p t n", t=T), kk,
                                       q_buf[n % KB][0:w, :].rearrange("p (t n) -> p t n", t=T), ALU.mult))
                eng.tensor_reduce(st[0:w, g, :].rearrange("p (h b t) -> p b t h", h=H, b=B)[:, b],
                                  prod[0:w, :].rearrange("p (t h d) -> p t h d", t=T, h=H), AX, ALU.add
                                  ).then_inc(s_sco, 1)

            def add_parts(bank, width):
                link(eng.tensor_copy(part[:, 0:width], bank[0:NS, 0:width]))
                for c0 in (NS, 2 * NS, 3 * NS):
                    last = eng.tensor_tensor(part[:, 0:width], bank[c0:c0 + NS, 0:width], part[:, 0:width], ALU.add)
                    if c0 < 3 * NS:
                        link(last)
                return last

            scored = 0
            for c in range(8):
                for j, tt in enumerate(ORDER if c < 6 else range(3)):
                    n = nt(tt)
                    z = 5 * c + j if c < 6 else 30 + 3 * (c - 6) + j
                    if j - 1 in ada_after(c):
                        ada_evac(ADA_1 + 2 * c + ada_after(c).index(j - 1))
                    if z < 30 and tt == SAMPLE:
                        eng.wait_ge(s_pj, pj_done(z))
                        if c == 5:
                            eng.wait_ge(s_pjv, 1)
                        add_parts(pb[z % 2], PJ_W).then_inc(s_part, 1)
                        eng.wait_ge(s_part, c + 1)
                    if z < 20:
                        i = z % 2
                        whole = part if tt == SAMPLE else pb[i][0:n, 0:PJ_W]
                        eng.wait_ge(s_sq, z + 1)
                        link(eng.tensor_reduce(ssq[i][0:n, :], sq[i][0:n, :].rearrange("p (h d) -> p h d", d=DH), AX,
                                               ALU.add))
                        eng.tensor_scalar(ssq[i][0:n, :], ssq[i][0:n, :], 1.0 / DH, EPS, ALU.mult, ALU.add
                                          ).then_inc(s_var, 1)
                        eng.wait_ge(s_sd, z + 1)
                        link(eng.reciprocal(ssq[i][0:n, :], ssq[i][0:n, :]))
                        if z >= 3:
                            eng.wait_ge(s_qkp, z - 2)
                            sem_out, val = KN_OUT[z - 3]
                            if sem_out is not None:
                                eng.wait_ge(s_qout if sem_out == "q" else s_kout[sem_out], val)
                        rows = kn[z % 3][0:n, :].rearrange("p (h d) -> p h d", d=DH)
                        eng.tensor_tensor(rows, whole.rearrange("p (h d) -> p h d", d=DH),
                                          ssq[i][0:n, :].unsqueeze(2).to_broadcast([n, 6, DH]), ALU.mult
                                          ).then_inc(s_pjq, 1)
                        eng.wait_ge(s_pjq, z + 1)
                        gain = (gq if c < 2 else gk)[0:n, :].unsqueeze(1).to_broadcast([n, 6, DH])
                        eng.tensor_tensor(rows, rows, gain, ALU.mult).then_inc(s_kn, 1)
                    elif z == 30:
                        link(eng.memset(upP[:, :, 0:2], 0.0))
                    elif z >= 34:
                        m = z - 34
                        eng.wait_ge(s_pj, pj_done(z))
                        eng.wait_ge(s_pjv, 14)
                        nat = upP[:, m, 2:2 + SEQ].rearrange("p (l r) -> p r l", r=DIL)
                        eng.tensor_tensor(nat, pb[z % 2][:, :].rearrange("p (r l) -> p r l", r=DIL),
                                          uT[:, m, 0:SEQ].rearrange("p (r l) -> p r l", r=DIL), ALU.mult)
                        eng.tensor_tensor(upS[:, m, :, 2:2 + T], pb[2 + z % 2][:, 0:NS].rearrange("p (b t) -> p b t", t=T),
                                          uT[:, m, SEQ:NTOK].rearrange("p (b t) -> p b t", t=T), ALU.mult
                                          ).then_inc(s_cmul, 1)
                    if 10 <= z < 34:
                        score(scored)
                        scored += 1
            assert scored == G * B
            eng.wait_ge(s_cmul, 2)
            for m in range(2):
                link(eng.tensor_copy(csx[:, m, 0:2], upP[:, m, SEQ:SEQ + 2]))
                eng.tensor_copy(csx[:, m, 2:18].rearrange("p (b j) -> p b j", j=2), upS[:, m, :, T:T + 2]
                                ).then_inc(s_csx, 1)
            eng.wait_ge(s_csx, 2)
            cp, cs_ = at(m_kn, SEQ), at(m_kn + SEQ, B, T)
            eng.wait_ge(s_qkp, 20)
            for i in range(3):
                eng.wait_ge(s_kout[i], KOUT[i])

            def convolve(m):
                w3 = t19[:, m, 16:19]
                link(eng.tensor_scalar(cp, upP[:, m, 0:SEQ], w3[:, 0:1], None, ALU.mult))
                link(eng.tensor_scalar(cs_, upS[:, m, :, 0:T], w3[:, 0:1], None, ALU.mult))
                for jj in (1, 2):
                    link(eng.scalar_tensor_tensor(out=cp, in0=upP[:, m, jj:jj + SEQ], scalar=w3[:, jj:jj + 1],
                                                  in1=cp, op0=ALU.mult, op1=ALU.add))
                    link(eng.scalar_tensor_tensor(out=cs_, in0=upS[:, m, :, jj:jj + T], scalar=w3[:, jj:jj + 1],
                                                  in1=cs_, op0=ALU.mult, op1=ALU.add))
                eng.tensor_tensor(catT[:, 6 + m, 0:SEQ].rearrange("p (r l) -> p r l", r=DIL),
                                  cp.rearrange("p (l r) -> p r l", r=DIL),
                                  gT[:, m, 0:SEQ].rearrange("p (r l) -> p r l", r=DIL), ALU.mult).then_inc(s_conv, 1)
                eng.tensor_tensor(catT[:, 6 + m, SEQ:NTOK], cs_.rearrange("p b t -> p (b t)"), gT[:, m, SEQ:NTOK],
                                  ALU.mult).then_inc(s_conv, 1)
                eng.wait_ge(s_conv, 2 * m + 2)
            eng.wait_ge(s_sS, 1)
            link(eng.tensor_tensor(sp[:], pb[7][:, 0:SW], ts[:], ALU.add))
            eng.tensor_reduce(snm, sp[:], AX, ALU.max, negate=True).then_inc(s_smx, 1)
            eng.wait_ge(s_sex, 1)
            link(eng.reciprocal(srz, szs))
            eng.tensor_scalar(sp[:], sp[:], srz, None, ALU.mult).then_inc(s_sP, 1)

            def norm(u):
                i = u % 2
                eng.wait_ge(s_ex, u + 1)
                link(eng.reciprocal(rz[:, i:i + 1], zs[:, i:i + 1]))
                eng.tensor_scalar(sc_t[i][:], sc_t[i][:], rz[:, i:i + 1], None, ALU.mult).then_inc(s_P, 1)

            def mask(m):
                if m >= 2:
                    eng.wait_ge(s_fold, m - 1)
                eng.tensor_tensor(vmul[m % 2], pb[2 * (m % 2) + 1][:, GW:2 * GW], headmask, ALU.mult).then_inc(s_mask, 1)

            eng.wait_ge(s_vm, 16)
            for u in range(18):
                if u >= 2:
                    eng.wait_ge(s_spv, SPV[VUNITS.index(WIDE[u - 2])])
                if u < 16:
                    h, r, i = u // 4, u % 4, u % 2
                    lo, hi = pb[2 * i], pb[2 * i + 1]
                    eng.wait_ge(s_S, u + 1)
                    if u >= 2:
                        eng.wait_ge(s_Tp, 2 * u - 2)
                    if r == 0:
                        eng.wait_ge(s_tb[h % 2], 48 * (h // 2 + 1))
                    tab = tb[h % 2]
                    eng.tensor_tensor(sc_t[i][:, 0:512].rearrange("p (a b) -> p a b", a=4),
                                      lo[:, :].rearrange("p (a b) -> p a b", a=4), tab[:, 3 - r:7 - r, :], ALU.add)
                    eng.tensor_tensor(sc_t[i][:, 512:768].rearrange("p (a b) -> p a b", a=2),
                                      hi[:, 0:256].rearrange("p (a b) -> p a b", a=2), tab[:, 7:9, :], ALU.add
                                      ).then_inc(s_add, 1)
                if 1 <= u <= 16:
                    norm(u - 1)
                if u < 16:
                    eng.wait_ge(s_add, u + 1)
                    eng.tensor_reduce(nmx[:, i:i + 1], sc_t[i][:], AX, ALU.max, negate=True).then_inc(s_mx, 1)
                if u >= 2:
                    mask(u - 2)
                if u in CONV:
                    convolve(CONV.index(u))

            def inverse_rms(j):
                tt = ORDER[j]
                n = nt(tt)
                eng.wait_ge(s_ss2, j + 1)
                eng.tensor_scalar(ss2[0:n, tt:tt + 1], ss2[0:n, tt:tt + 1], 1.0 / D, EPS, ALU.mult, ALU.add
                                  ).then_inc(s_var2, 1)
                eng.wait_ge(s_sd2, j + 1)
                link(eng.reciprocal(rs2[0:n, tt:tt + 1], rs2[0:n, tt:tt + 1]))
                if j == 0:
                    eng.wait_ge(s_m2, 16 * 2 * (T + 1))

            def second_norm(j):
                tt = ORDER[j]
                n, s = nt(tt), int(tt == SAMPLE)
                if j >= 2:
                    eng.wait_ge(s_h2p, 2 * j - 2)
                    eng.wait_ge(s_h2w[j % 2], 16 * (j // 2))
                link(eng.scalar_tensor_tensor(out=h2_row[j % 2][0:n, :], in0=x_t[0:n, tt, :], scalar=rs2[0:n, tt:tt + 1],
                                              in1=m2[s][1][0:n, :], op0=ALU.mult, op1=ALU.mult))
                eng.tensor_tensor(h2_row[j % 2][0:n, :], h2_row[j % 2][0:n, :], m2[s][2][0:n, :], ALU.add
                                  ).then_inc(s_h2, 1)

            eng.wait_ge(s_g1, 16 * (T + 1))
            for o in range(3):
                c0, w = sum(WO_W[:o]), WO_W[o]
                for j, tt in enumerate(ORDER):
                    u, n, s = 5 * o + j, nt(tt), int(tt == SAMPLE)
                    eng.wait_ge(s_wo, wo_done(u))
                    whole = pb[u % 2][0:n, 0:w]
                    if s:
                        link(add_parts(pb[u % 2], w))
                        whole = part[:, 0:w]
                    eng.tensor_tensor(wt[u % 2][0:n, 0:w], whole, m2[s][0][0:n, c0:c0 + w], ALU.mult).then_inc(s_wg, 1)
                    eng.wait_ge(s_wg, u + 1)
                    eng.tensor_tensor(x_t[0:n, tt, c0:c0 + w], x_t[0:n, tt, c0:c0 + w], wt[u % 2][0:n, 0:w], ALU.add
                                      ).then_inc(s_x1, 1)
                    if u in (12, 13):
                        inverse_rms(u - 12)
                        second_norm(u - 12)
            eng.wait_ge(s_vout, 16 * (DIL * G + 1))
            link(eng.memset(r_m, 0.0))
            eng.memset(r_sc, 0.0).then_inc(s_rz, 1)
            for j in range(2, TILES):
                inverse_rms(j)
            for j in range(2, TILES):
                second_norm(j)
            link(eng.tensor_copy(slotb[:, 0:15], const("slot")[:, 0:15]))
            eng.wait_ge(s_sc, TILES)

            def r3(v):
                return v.rearrange("p (k n) -> p k n", k=TILES)
            link(eng.tensor_tensor(r3(r_sel), r3(r_sc), br[:].unsqueeze(1).to_broadcast([P, TILES, NE]), ALU.add))
            for q in range(TILES * 8):
                last = eng.max(r_t8[:, 8 * q:8 * q + 8], r_sel[:, 8 * q:8 * q + 8])
            link(last)
            t8 = r_t8.rearrange("p (q n) -> p q n", n=8)
            link(eng.tensor_tensor(r_gs, t8[:, :, 0], t8[:, :, 1], ALU.add))
            gs = r_gs.rearrange("p (k g) -> p k g", k=TILES)
            other = gs.unsqueeze(2).to_broadcast([P, TILES, 8, 8])
            own = gs.unsqueeze(3).to_broadcast([P, TILES, 8, 8])

            def r4(v):
                return v.rearrange("p (k g h) -> p k g h", k=TILES, g=8)
            link(eng.tensor_tensor(r4(r_gt), other, own, ALU.is_gt))
            link(eng.tensor_tensor(r4(r_eq), other, own, ALU.is_equal))
            link(eng.tensor_tensor(r3(r_eq), r3(r_eq), const("tri8").unsqueeze(1).to_broadcast([P, TILES, 64]), ALU.mult))
            link(eng.tensor_tensor(r_gt, r_gt, r_eq, ALU.add))
            link(eng.tensor_reduce(r_rank, r_gt.rearrange("p (q n) -> p q n", n=8), AX, ALU.add))
            link(eng.tensor_scalar(r_gmb, r_rank, 3.5, NEG, ALU.is_ge, ALU.mult))
            link(eng.tensor_tensor(r_ma.rearrange("p (q n) -> p q n", n=8), r_sel.rearrange("p (q n) -> p q n", n=8),
                                   r_gmb.unsqueeze(2).to_broadcast([P, TILES * 8, 8]), ALU.add))
            for k in range(TILES):
                last = eng.max(r_top[:, k, :], r_ma[:, NE * k:NE * (k + 1)])
            link(last)
            for k in range(TILES):
                last = eng.match_replace(r_mr[:, NE * k:NE * (k + 1)], r_top[:, k, :], r_ma[:, NE * k:NE * (k + 1)], 2 * NEG)
            link(last)
            eng.tensor_tensor(r_m[:, 0:SAMPLE * NE], r_ma[:, 0:SAMPLE * NE], r_mr[:, 0:SAMPLE * NE], ALU.not_equal)
            eng.tensor_tensor(r_m[0:NS, SAMPLE * NE:RW], r_ma[0:NS, SAMPLE * NE:RW], r_mr[0:NS, SAMPLE * NE:RW],
                              ALU.not_equal).then_inc(s_M, 1)
            eng.wait_ge(s_M, 1)

            def shared_mul(f):
                eng.wait_ge(s_su, 2 * f + 2)
                eng.wait_ge(s_sg, f + 1)
                eng.tensor_tensor(hs[:, f, 0:SEQ], pb[4 * f + 1][:, :], sg[:, f, 0:SEQ], ALU.mult)
                eng.tensor_tensor(hs[:, f, SEQ:NTOK], pb[4 * f + 3][:, 0:NS], sg[:, f, SEQ:NTOK], ALU.mult
                                  ).then_inc(s_hs, 1)
            shared_mul(0)
            link(eng.tensor_tensor(r_g, r_sc, r_m, ALU.mult))
            link(eng.tensor_reduce(r_den, r3(r_g), AX, ALU.add))
            link(eng.tensor_scalar(r_den, r_den, 1e-30, None, ALU.max))
            link(eng.reciprocal(r_den, r_den))
            link(eng.tensor_scalar(r_den, r_den, 2.5, None, ALU.mult))
            eng.tensor_tensor(r3(r_g), r3(r_g), r_den.unsqueeze(2).to_broadcast([P, TILES, NE]), ALU.mult
                              ).then_inc(s_G, 1)
            eng.wait_ge(s_rank, 1)
            link(eng.tensor_copy(r_cnt, pb[3][:, RW:RW + NE]))
            link(eng.tensor_scalar(r_nt, r_cnt, 0.0, None, ALU.is_gt))
            for k in range(1, TILES):
                link(eng.scalar_tensor_tensor(out=r_nt, in0=r_cnt, scalar=float(P * k), in1=r_nt, op0=ALU.is_gt,
                                              op1=ALU.add))
            link(eng.tensor_tensor_scan(r_incl, const("ones")[:, 0:NE], r_nt, 0.0, ALU.mult, ALU.add))
            link(eng.tensor_scalar(r_cmp, r_incl, const("iotacol"), None, ALU.is_le))
            link(eng.tensor_reduce(ecol[:], r_cmp, AX, ALU.add))
            link(eng.tensor_scalar(ecol[:], ecol[:], float(NE - 1), None, ALU.min))
            link(eng.tensor_scalar(fpair, const("iota", parts=1), float(ET), r_incl[0:1, NE - 1:NE], ALU.mult, ALU.is_lt))
            link(eng.tensor_reduce(fcnt[:], fpair, AX, ALU.add))
            link(eng.tensor_copy(meta[0:1, P:P + 1], fcnt[:]))
            link(eng.tensor_tensor(r_base, r_incl, r_nt, ALU.subtract))
            link(eng.tensor_scalar(r_base, r_base, float(P), 1.0, ALU.mult, ALU.add))
            link(eng.tensor_tensor(r3(r_pos), pb[3][:, 0:RW].rearrange("p (k n) -> p k n", k=TILES),
                                   r_base.unsqueeze(1).to_broadcast([P, TILES, NE]), ALU.add))
            eng.nop().then_inc(s_ecol, 1)
            link(eng.tensor_tensor(r_pos, r_pos, r_m, ALU.mult))
            link(eng.tensor_scalar(r_pos, r_pos, -1.0, None, ALU.add))
            eng.wait_ge(s_eT, 1)
            eng.tensor_copy(meta[0:1, 0:P], pb[3][0:1, RW:RW + P]).then_inc(s_meta, 1)
            eng.wait_ge(s_meta, 1)
            groups = eng.value_load(meta[0:1, P:P + 1], min_val=1, max_val=P // ET - 1)

            def one_hot(s, t):
                e = eng.value_load(meta[0:1, bass.ds(t, 1)], min_val=0, max_val=NE - 1)
                for k in range(TILES):
                    last = eng.tensor_scalar(oneh[s][:, k, :], const("iota"), r_pos[:, bass.ds(e + NE * k, 1)],
                                             const("negt")[:, bass.ds(t, 1)], ALU.subtract, ALU.is_equal)
                last.then_inc(s_oneh, 1)

            def rows(s, t):
                eng.wait_ge(s_im, t + 1)
                link_rows(eng.tensor_scalar(imt[:, 0:1], pb[6][:, 2:3], const("negdummy"), const("dummy"), ALU.mult,
                                            ALU.add), 2 * t + 1)
                link_rows(eng.tensor_tensor(imt[:, 1:2], imt[:, 0:1], pb[6][:, 0:1], ALU.add), 2 * t + 2)
                eng.tensor_tensor(ix[s], imt[:, 1:2], pb[6][:, 1:2], ALU.add).then_inc(s_ix, 1)

            def link_rows(ins, count):
                ins.then_inc(s_lrow, 1)
                eng.wait_ge(s_lrow, count)

            def x_evac(s, t, uses):
                eng.wait_ge(s_tp, 2 * t + 2)
                eng.tensor_copy(xT[s][:, 4:8, :], pb[5][:, :].rearrange("p (k n) -> p k n", k=4)).then_inc(s_xd, 1)
                e = eng.value_load(meta[0:1, bass.ds(t, 1)], min_val=0, max_val=NE - 1)
                eng.wait_ge(s_ga[s], 16 * uses)
                if not isinstance(t, int):
                    eng.wait_ge(s_ya, t)
                eng.tensor_copy(gcol[s], xg[s][:, bass.ds(e + D, 1)]).then_inc(s_gc, 1)

            one_hot(0, 0)
            one_hot(1, 1)
            shared_mul(1)
            rows(0, 0)
            rows(1, 1)
            x_evac(0, 0, 1)
            eng.nop().then_inc(s_he, 1)
            eng.nop().then_inc(s_yd, 1)
            eng.tensor_copy(ixs[0], ix[0]).then_inc(s_ixs, 1)
            for i in range(2):
                eng.wait_ge(s_yw[i], 16 * (3 - i))
            with eng.Fori(0, groups) as i:
                for s in range(ET):
                    t = ET * i + s
                    one_hot(s, t + 2)
                    eng.wait_ge(s_up, ET + t + 1)
                    eng.wait_ge(s_si, t + 1)
                    eng.wait_ge(s_dn, 2 * ET + 2 * t - 2)
                    eng.tensor_tensor(he[s], pb[1][:, 0:2 * P].rearrange("p (f n) -> p f n", f=2), sge[s], ALU.mult
                                      ).then_inc(s_he, 1)
                    rows(s, t + 2)
                    x_evac(1 - s, t + 1, i + 1 + s)
                    eng.wait_ge(s_dn, 2 * ET + 2 * t + 2)
                    eng.tensor_scalar(yo[s][:, 512:D], pb[3][:, :], gcol[s], None, ALU.mult).then_inc(s_yd, 1)
                    eng.wait_ge(s_sca, 16 * t + 16)
                    eng.tensor_copy(ixs[1 - s], ix[1 - s]).then_inc(s_ixs, 1)
            eng.wait_ge(s_g2, 16 * (T + 1))
            for j, tt in enumerate(ORDER):
                n, s = nt(tt), int(tt == SAMPLE)
                eng.wait_ge(s_yf[tt], 16)
                link(eng.tensor_tensor(yf[tt][0:n, :], yf[tt][0:n, :], g2[s][0:n, :], ALU.mult))
                eng.tensor_tensor(yf[tt][0:n, :], yf[tt][0:n, :], x_t[0:n, tt, :], ALU.add).then_inc(s_fin, 1)


_OUTS = ([(1, SEQ, D), (B, T, D)] + [(1, 1, min(w, SEQ), H, DH) for w in (128, 128, 512, 512, 2048, 2048)]
         + [(1, 1, 2, CC)] + [(1, B, min(w, 1024), H, DH) for w in (128, 128, 512, 512, 2048, 2048)]
         + [(1, B, 2, CC)])


def kernel(**inputs):
    import concourse.bacc as bacc
    from concourse.bass_utils import run_bass_kernel_spmd

    nc = bacc.Bacc("TRN2", target_bir_lowering=False, num_devices=1)
    arrays = {n: np.ascontiguousarray(x) for n, x in inputs.items()}
    arrays.update(constants())
    aps = {}
    feeds = {}
    for n, x in arrays.items():
        feeds[f"in_{n}"] = x
        aps[n] = nc.dram_tensor(f"in_{n}", x.shape, mybir.dt.from_np(x.dtype), kind="ExternalInput").ap()
    outs = [nc.dram_tensor(f"out_{i}", s, F32, kind="ExternalOutput").ap() for i, s in enumerate(_OUTS)]
    build(nc, aps, outs)
    r = run_bass_kernel_spmd(nc, [feeds], core_ids=[0])
    return tuple(r.results[0][f"out_{i}"] for i in range(len(_OUTS)))
```
